# Optimizing a Trainium2 kernel written in Bass

```python
import jax, jax.numpy as jnp
from jax import lax
import numpy as np

D_MODEL = 1024
BATCH = 1
SEQ = 512
DEPTH = 2

MEM_LEN = 256
RET_HEADS = 4
RET_DK = 64
RET_DV = 128
RET_CHUNK = 256
MOBA_HEADS = 4
MOBA_DH = 64
MOBA_BLOCK = 256
MOBA_TOPK = 3
MOBA_QCHUNK = 32
MEM_HEADS = 4
MEM_DH = 64
N_GROUPS = 4
EXPERTS_PER_GROUP = 4
N_EXPERTS = N_GROUPS * EXPERTS_PER_GROUP
TOPK_IN_GROUP = 2
EXPERT_FF = 512
EPS = 1e-6
PAD_MULT = 256

RET_QK = RET_HEADS * RET_DK
RET_V = RET_HEADS * RET_DV
MOBA_W = MOBA_HEADS * MOBA_DH
MEM_W = MEM_HEADS * MEM_DH
D_MIX = RET_V + MOBA_W + MEM_W
IN_SPLITS = [RET_QK, RET_QK, RET_V, RET_V, MOBA_W, MOBA_W, MOBA_W, MEM_W]
D_IN = sum(IN_SPLITS)
SPLIT_POINTS = [int(v) for v in np.cumsum(IN_SPLITS)[:-1]]

kernel_name = "hymba_retention_moba_memory_hmoe"

def rms_norm(x, g):
    xf = x.astype(jnp.float32)
    y = xf * lax.rsqrt(jnp.mean(xf * xf, axis=-1, keepdims=True) + EPS)
    return (y * g.astype(jnp.float32)).astype(x.dtype)

def split_heads(t, n_heads):
    b, s, _ = t.shape
    return t.reshape(b, s, n_heads, -1).transpose(0, 2, 1, 3)

def merge_heads(t):
    b, h, s, d = t.shape
    return t.transpose(0, 2, 1, 3).reshape(b, s, h * d)

def pad_seq(t, s_pad):
    return jnp.pad(t, ((0, 0), (0, 0), (0, s_pad - t.shape[2]), (0, 0)))

def rotary(t, pos):
    half = t.shape[-1] // 2
    inv = 1.0 / (10000.0 ** jnp.linspace(0.0, 1.0, half, dtype=jnp.float32))
    ang = pos.astype(jnp.float32)[:, None] * inv[None, :]
    cos = jnp.cos(ang).astype(t.dtype)
    sin = jnp.sin(ang).astype(t.dtype)
    t1, t2 = t[..., :half], t[..., half:]
    return jnp.concatenate([t1 * cos - t2 * sin, t1 * sin + t2 * cos], axis=-1)

def retention(q, k, v):
    b, h, s, dk = q.shape
    dv = v.shape[-1]
    c = RET_CHUNK
    nc = s // c
    dt = q.dtype
    log_g = jnp.log1p(-(2.0 ** (-5.0 - jnp.arange(h, dtype=jnp.float32))))
    n = jnp.arange(c, dtype=jnp.float32)
    diff = n[:, None] - n[None, :]
    dmask = jnp.where(diff >= 0, jnp.exp(log_g[:, None, None] * jnp.maximum(diff, 0.0)), 0.0)
    q_decay = jnp.exp(log_g[:, None] * (n + 1.0))
    k_decay = jnp.exp(log_g[:, None] * (c - 1.0 - n))
    chunk_decay = jnp.exp(log_g * c).astype(dt)
    qc = q.reshape(b, h, nc, c, dk)
    kc = k.reshape(b, h, nc, c, dk)
    vc = v.reshape(b, h, nc, c, dv)
    scores = jnp.einsum('bhncd,bhnmd->bhncm', qc, kc) * dmask[None, :, None].astype(dt)
    o_intra = jnp.einsum('bhncm,bhnmv->bhncv', scores, vc)
    upd = jnp.einsum('bhnmd,bhnmv->bhndv', kc * k_decay[None, :, None, :, None].astype(dt), vc)

    def step(state, u):
        return state * chunk_decay[None, :, None, None] + u, state

    _, r_prev = lax.scan(step, jnp.zeros((b, h, dk, dv), dt), jnp.moveaxis(upd, 2, 0))
    r_prev = jnp.moveaxis(r_prev, 0, 2)
    o_cross = jnp.einsum('bhncd,bhndv->bhncv', qc * q_decay[None, :, None, :, None].astype(dt), r_prev)
    return (o_intra + o_cross).reshape(b, h, s, dv)

def moba_attention(q, k, v):
    b, h, s, d = q.shape
    nb = s // MOBA_BLOCK
    kk = min(MOBA_TOPK, nb)
    scale = d ** -0.5
    kb = k.reshape(b, h, nb, MOBA_BLOCK, d)
    vb = v.reshape(b, h, nb, MOBA_BLOCK, d)
    kmean = jnp.mean(kb.astype(jnp.float32), axis=3).astype(k.dtype)
    n_qc = s // MOBA_QCHUNK
    q_chunks = jnp.moveaxis(q.reshape(b, h, n_qc, MOBA_QCHUNK, d), 2, 0)
    bi = jnp.arange(b)[:, None, None, None]
    hi = jnp.arange(h)[None, :, None, None]

    def one_chunk(args):
        qc, ci = args
        start = ci * MOBA_QCHUNK
        blk = start // MOBA_BLOCK
        qpos = start + jnp.arange(MOBA_QCHUNK)
        gate = jnp.einsum('bhqd,bhnd->bhqn', qc, kmean).astype(jnp.float32)
        gate = jnp.where(jnp.arange(nb) < blk, gate, -jnp.inf)
        _, idx = lax.top_k(gate, kk)
        valid = idx < blk
        k_sel = kb[bi, hi, idx]
        v_sel = vb[bi, hi, idx]
        s_sel = jnp.einsum('bhqd,bhqjtd->bhqjt', qc, k_sel).astype(jnp.float32) * scale
        s_sel = jnp.where(valid[..., None], s_sel, -jnp.inf).reshape(b, h, MOBA_QCHUNK, kk * MOBA_BLOCK)
        k_own = lax.dynamic_index_in_dim(kb, blk, axis=2, keepdims=False)
        v_own = lax.dynamic_index_in_dim(vb, blk, axis=2, keepdims=False)
        s_own = jnp.einsum('bhqd,bhtd->bhqt', qc, k_own).astype(jnp.float32) * scale
        kpos = blk * MOBA_BLOCK + jnp.arange(MOBA_BLOCK)
        s_own = jnp.where(kpos[None, :] <= qpos[:, None], s_own, -jnp.inf)
        p = jax.nn.softmax(jnp.concatenate([s_sel, s_own], axis=-1), axis=-1).astype(qc.dtype)
        o = jnp.einsum('bhqs,bhqsd->bhqd', p[..., :kk * MOBA_BLOCK],
                       v_sel.reshape(b, h, MOBA_QCHUNK, kk * MOBA_BLOCK, d))
        return o + jnp.einsum('bhqt,bhtd->bhqd', p[..., kk * MOBA_BLOCK:], v_own)

    out = lax.map(one_chunk, (q_chunks, jnp.arange(n_qc)))
    return jnp.moveaxis(out, 0, 2).reshape(b, h, s, d)

def memory_attention(q, mk, mv):
    s = jnp.einsum('bhsd,bhmd->bhsm', q, mk).astype(jnp.float32) * (q.shape[-1] ** -0.5)
    p = jax.nn.softmax(s, axis=-1).astype(q.dtype)
    return jnp.einsum('bhsm,bhmd->bhsd', p, mv)

def hier_moe(x, w_grp, b_grp, w_exp, b_exp, w_gate, w_up, w_down):
    b, s, d = x.shape
    t = x.reshape(b * s, d)
    g_prob = jax.nn.softmax((t @ w_grp + b_grp).astype(jnp.float32), axis=-1)
    g_w, g_idx = lax.top_k(g_prob, 1)
    e_logits = (t @ w_exp + b_exp).astype(jnp.float32).reshape(b * s, N_GROUPS, EXPERTS_PER_GROUP)
    e_in = jnp.take_along_axis(e_logits, g_idx[:, :, None], axis=1)[:, 0]
    e_prob = jax.nn.softmax(e_in, axis=-1)
    e_w, e_idx = lax.top_k(e_prob, TOPK_IN_GROUP)
    e_w = e_w / jnp.sum(e_w, axis=-1, keepdims=True)
    weights = g_w * e_w
    expert_id = g_idx * EXPERTS_PER_GROUP + e_idx
    combine = jnp.sum(jax.nn.one_hot(expert_id, N_EXPERTS, dtype=jnp.float32) * weights[..., None], axis=1)
    combine = combine.astype(t.dtype)
    out = jnp.zeros_like(t)
    for e in range(N_EXPERTS):
        hid = jax.nn.silu(t @ w_gate[e]) * (t @ w_up[e])
        out = out + combine[:, e:e + 1] * (hid @ w_down[e])
    return out.reshape(b, s, d)

def setup_inputs(seed: int = 0) -> dict:
    key = jax.random.key(seed)
    ks = jax.random.split(key, 24)
    f32 = jnp.float32

    def nrm(k, shape, fan_in):
        return jax.random.normal(k, shape, f32) * (fan_in ** -0.5)

    def gain(k, shape):
        return 1.0 + 0.02 * jax.random.normal(k, shape, f32)

    return {
        "x": jax.random.normal(ks[0], (BATCH, SEQ, D_MODEL), f32),
        "mem": jax.random.normal(ks[1], (BATCH, MEM_LEN, D_MODEL), f32),
        "norm1_g": gain(ks[2], (DEPTH, D_MODEL)),
        "w_in": nrm(ks[3], (DEPTH, D_MODEL, D_IN), D_MODEL),
        "ret_norm_g": gain(ks[4], (DEPTH, RET_HEADS, RET_DV)),
        "moba_qn_g": gain(ks[5], (DEPTH, MOBA_DH)),
        "moba_kn_g": gain(ks[6], (DEPTH, MOBA_DH)),
        "mem_norm_g": gain(ks[7], (DEPTH, D_MODEL)),
        "w_mem_kv": nrm(ks[8], (DEPTH, D_MODEL, 2 * MEM_W), D_MODEL),
        "mem_qn_g": gain(ks[9], (DEPTH, MEM_DH)),
        "mem_kn_g": gain(ks[10], (DEPTH, MEM_DH)),
        "w_out": nrm(ks[11], (DEPTH, D_MIX, D_MODEL), D_MIX),
        "norm2_g": gain(ks[12], (DEPTH, D_MODEL)),
        "w_router_grp": nrm(ks[13], (DEPTH, D_MODEL, N_GROUPS), D_MODEL),
        "b_router_grp": 0.01 * jax.random.normal(ks[14], (DEPTH, N_GROUPS), f32),
        "w_router_exp": nrm(ks[15], (DEPTH, D_MODEL, N_EXPERTS), D_MODEL),
        "b_router_exp": 0.01 * jax.random.normal(ks[16], (DEPTH, N_EXPERTS), f32),
        "w_exp_gate": nrm(ks[17], (DEPTH, N_EXPERTS, D_MODEL, EXPERT_FF), D_MODEL),
        "w_exp_up": nrm(ks[18], (DEPTH, N_EXPERTS, D_MODEL, EXPERT_FF), D_MODEL),
        "w_exp_down": nrm(ks[19], (DEPTH, N_EXPERTS, EXPERT_FF, D_MODEL), EXPERT_FF),
    }

def reference(x, mem, norm1_g, w_in, ret_norm_g, moba_qn_g, moba_kn_g, mem_norm_g, w_mem_kv,
              mem_qn_g, mem_kn_g, w_out, norm2_g, w_router_grp, b_router_grp, w_router_exp,
              b_router_exp, w_exp_gate, w_exp_up, w_exp_down):
    b, s, _ = x.shape
    s_pad = -(-s // PAD_MULT) * PAD_MULT
    pos = jnp.arange(s)
    for l in range(DEPTH):
        h = rms_norm(x, norm1_g[l])
        proj = h @ w_in[l]
        r_q, r_k, r_v, r_g, m_q, m_k, m_v, c_q = jnp.split(proj, SPLIT_POINTS, axis=-1)

        rq = rotary(split_heads(r_q, RET_HEADS), pos)
        rk = rotary(split_heads(r_k, RET_HEADS), pos) * (RET_DK ** -0.5)
        rv = split_heads(r_v, RET_HEADS)
        ro = retention(pad_seq(rq, s_pad), pad_seq(rk, s_pad), pad_seq(rv, s_pad))[:, :, :s]
        ro = rms_norm(ro, ret_norm_g[l][:, None, :])
        y_ret = jax.nn.silu(r_g) * merge_heads(ro)

        mq = rms_norm(split_heads(m_q, MOBA_HEADS), moba_qn_g[l])
        mk = rms_norm(split_heads(m_k, MOBA_HEADS), moba_kn_g[l])
        mv = split_heads(m_v, MOBA_HEADS)
        mo = moba_attention(pad_seq(mq, s_pad), pad_seq(mk, s_pad), pad_seq(mv, s_pad))[:, :, :s]
        y_moba = merge_heads(mo)

        mem_kv = rms_norm(mem, mem_norm_g[l]) @ w_mem_kv[l]
        ck = rms_norm(split_heads(mem_kv[..., :MEM_W], MEM_HEADS), mem_kn_g[l])
        cv = split_heads(mem_kv[..., MEM_W:], MEM_HEADS)
        cq = rms_norm(split_heads(c_q, MEM_HEADS), mem_qn_g[l])
        y_mem = merge_heads(memory_attention(cq, ck, cv))

        x = x + jnp.concatenate([y_ret, y_moba, y_mem], axis=-1) @ w_out[l]

        x = x + hier_moe(rms_norm(x, norm2_g[l]), w_router_grp[l], b_router_grp[l],
                         w_router_exp[l], b_router_exp[l], w_exp_gate[l], w_exp_up[l], w_exp_down[l])
    return x


_drawn_inputs = setup_inputs


def setup_inputs(seed=0):
    import zlib

    import numpy as np

    out = dict(_drawn_inputs(seed))
    spreads = {}
    factors = {'moba_qn_g': 4.79,
     'moba_kn_g': 4.806,
     'mem_norm_g': 5.296,
     'mem_qn_g': 7.809,
     'mem_kn_g': 8.0,
     'b_router_exp': 3.018,
     'ret_norm_g': 2.91}
    for name, (base, spread) in spreads.items():
        noise = np.random.default_rng([zlib.crc32(name.encode()), seed]).standard_normal(out[name].shape)
        drawn = base * np.exp(spread * noise) if base else spread * noise
        out[name] = __import__('jax').numpy.asarray(drawn.astype(out[name].dtype))
    for name, factor in factors.items():
        out[name] = (out[name] * factor).astype(out[name].dtype)
    return out
```

```python
import concourse.bass as bass
from concourse import mybir
from contextlib import ExitStack

DEPTH, SEQ, D, MEM = 2, 512, 1024, 256
D_IN, E_N, FF = 2560, 16, 512
NT = SEQ // 128
KT = D // 128
FT = FF // 128
H, DH = 4, 64
CH = 512
NS, NW = 8, 4
U_MEM, U_PROJ, U_OUT = 4, 20, 8
U_ATT = U_MEM + U_PROJ + U_OUT
U_E = 12
U_PASS = U_E * E_N
CHUNKS = [3, 4, 0, 1, 2]
NEG = -3.0e38
EMPTY = 1.0e6
CONST = dict(ident=128, cos=128, sin=128, dmask=1024, qdec=512, kdec=8, causal=128, below=128,
             ones=128, iota=16, pairid=8, empty=128, limits=3, eps=1)
OFF, _o = {}, 0
for _k, _v in CONST.items():
    OFF[_k] = _o
    _o += _v
N_CONST = _o


def build(nc, a, out):
    f32, f32r, bf16 = mybir.dt.float32, mybir.dt.float32r, mybir.dt.bfloat16
    i32, u32 = mybir.dt.int32, mybir.dt.uint32
    ACT, ALU, AX = mybir.ActivationFunctionType, mybir.AluOpType, mybir.AxisListType
    ctx = ExitStack()
    with ctx:
        def sb(name, shape, dt=f32, scope=ctx):
            return scope.enter_context(nc.sbuf_tensor(name, shape, dt))

        x = sb("x", [128, NT, D])
        stage = sb("stage", [128, NS, D])
        w_hi = sb("w_hi", [128, NW, D], f32r)
        w_lo = sb("w_lo", [128, NW, D], f32r)
        hT_hi = sb("hT_hi", [128, KT, SEQ], f32r)
        hT_lo = sb("hT_lo", [128, KT, SEQ], f32r)
        act = sb("act", [128, NT, D])
        gvec = sb("gvec", [128, D])
        con = sb("con", [128, N_CONST])
        g_ret = sb("g_ret", [128, H * 128])
        g_head = sb("g_head", [128, 4, DH])
        r_bias = sb("r_bias", [128, 4 + E_N])
        wr = sb("wr", [128, KT, 20])
        wr_hi = sb("wr_hi", [128, KT, 20], f32r)
        wr_lo = sb("wr_lo", [128, KT, 20], f32r)
        ss = sb("ss", [128, 16])
        rstd = sb("rstd", [128, 16])
        ssq = sb("ssq", [128, 32 + 16 + 8])
        rstdq = sb("rstdq", [128, 56])
        ssr = sb("ssr", [128, 16])
        rstdr = sb("rstdr", [128, 16])
        mx = sb("mx", [128, 2])
        nmx = sb("nmx", [128, 2, 2])
        rsum = sb("rsum", [128, NT, 8])
        rinv = sb("rinv", [128, NT, 8])
        lg = sb("lg", [128, NT, 20])
        gp = sb("gp", [128, NT, 8])
        ep = sb("ep", [128, NT, 8])
        top = sb("top", [128, NT, 8])
        topi = sb("topi", [128, NT, 8], u32)
        gnum = sb("gnum", [128, NT])
        gexp = sb("gexp", [128, NT, 4])
        gw = sb("gw", [128, NT])
        oneg = sb("oneg", [128, NT, 4])
        prod = sb("prod", [128, NT, 16])
        td = sb("td", [128, NT])
        te = sb("te", [128, NT])
        wtok = sb("wtok", [128, 2, NT])
        enum = sb("enum", [128, 2, NT])
        one_e = sb("one_e", [128, 2, NT, 16])
        sel = sb("sel", [128, NT, 16])
        pos = sb("pos", [128, 2, NT])
        row_i = sb("row_i", [128, 2, NT], i32)
        tmpr = sb("tmpr", [128, 4])
        rounds_i = sb("rounds_i", [128, 1], i32)
        tab = sb("tab", [64, 128])
        slot_tok = sb("slot_tok", [128, 64], i32)
        slot_pair = sb("slot_pair", [128, 64], i32)
        pair_f = sb("pair_f", [128, 64])
        tok_f = sb("tok_f", [128, 64])
        tok_now = sb("tok_now", [128, 2, 1], i32)
        pair_now = sb("pair_now", [128, 2, 1], i32)

        def const(name, parts=128):
            return con[0:parts, OFF[name]:OFF[name] + CONST[name]]

        ident = const("ident")
        cos_t = const("cos").rearrange("p (t c) -> p t c", t=NT)
        sin_t = const("sin").rearrange("p (t c) -> p t c", t=NT)
        dmask = const("dmask").rearrange("p (h c) -> p h c", h=H)
        qdec = const("qdec").rearrange("p (g c) -> p g c", g=2)
        kdec = const("kdec").rearrange("p (t h) -> p t h", t=2)
        eps = const("eps")

        with ExitStack() as part:
            pq = {c: sb(f"proj{c}", [128, NT, CH], scope=part) for c in (0, 1, 4, 3)}
            pq[2] = pq[3]
            hd = sb("hd", [128, 3, 2, SEQ], scope=part)
            ckT = sb("ckT", [128, 2, MEM], scope=part)
            probs = sb("probs", [128, 2, 512], scope=part)
            probsT = sb("probsT", [128, 2, 512], scope=part)
            cv = sb("cv", [128, 2, H * DH], scope=part)
        with ExitStack() as part:
            mT_hi = sb("mT_hi", [128, KT, MEM], f32r, scope=part)
            mT_lo = sb("mT_lo", [128, KT, MEM], f32r, scope=part)
        with ExitStack() as part:
            xg = sb("xg", [128, 2, D], scope=part)
            xgT_hi = sb("xgT_hi", [128, 2, KT, 128], f32r, scope=part)
            xgT_lo = sb("xgT_lo", [128, 2, KT, 128], f32r, scope=part)
            sil = sb("sil", [128, FF], scope=part)
            hid = sb("hid", [128, FF], scope=part)
            hidT_hi = sb("hidT_hi", [128, FT, 128], f32r, scope=part)
            hidT_lo = sb("hidT_lo", [128, FT, 128], f32r, scope=part)
            ysb = sb("ysb", [128, 2, D], scope=part)
        ck = probsT
        junk = probs[:, 0, :].bitcast(bf16)
        sq = act[:, 2, 0:512]
        sqr = probs[:, 0, :]
        rot_a, rot_b = act[:, 0, 0:512], act[:, 1, 0:512]
        kd = act[:, 3, 0:512].rearrange("p (t c) -> p t c", t=2)
        qdT = hd[:, 2, :, 0:256]
        state = hd[:, 2, :, 256:512]

        bank = [ctx.enter_context(nc.psum_tensor(f"bank{i}", [128, 512], f32)) for i in range(8)]

        h2_d = nc.dram_tensor("h2_scratch", (SEQ, D), f32).ap()
        tab_d = nc.dram_tensor("slot_table", (E_N * SEQ, 1), f32).ap()
        y_d = nc.dram_tensor("pair_rows", (2 * SEQ, D), f32).ap()

        def sem(name):
            return ctx.enter_context(nc.semaphore(name))

        s_const = sem("s_const")
        s_pad = sem("s_pad")
        s_xin = sem("s_xin")
        s_stage = [sem(f"s_stage{i}") for i in range(NS)]
        s_hi = sem("s_hi")
        s_lo = sem("s_lo")
        s_used = sem("s_used")
        s_x = sem("s_x")
        s_rounds = sem("s_rounds")
        s_arrive = sem("s_arrive")
        s_apart = sem("s_apart")
        s_go = sem("s_go")
        s_out = sem("s_out")
        s_memx = sem("s_memx")
        s_gain = [sem(f"s_gain{i}") for i in range(3)]
        s_small = sem("s_small")
        s_wr = sem("s_wr")
        s_tabi = sem("s_tabi")
        s_h2st = sem("s_h2st")
        s_tabw = sem("s_tabw")
        s_tabr = sem("s_tabr")
        s_xg = [sem(f"s_xg{i}") for i in range(2)]
        s_yst = [sem(f"s_yst{i}") for i in range(2)]
        s_yg = [sem(f"s_yg{i}") for i in range(4)]
        s_first = sem("s_first")
        s_known = sem("s_known")
        s_dve = sem("s_dve")
        s_act = sem("s_act")
        s_pool = sem("s_pool")
        s_wrh = sem("s_wrh")
        s_wrl = sem("s_wrl")
        s_std = sem("s_std")
        s_hm = sem("s_hm")
        s_h1 = sem("s_h1")
        s_tr = sem("s_tr")
        s_trh = sem("s_trh")
        s_trl = sem("s_trl")
        s_mkv = sem("s_mkv")
        s_mkve = sem("s_mkve")
        s_proj = sem("s_proj")
        s_pev = sem("s_pev")
        s_ssq = sem("s_ssq")
        s_stdq = sem("s_stdq")
        s_qn = sem("s_qn")
        s_tq = sem("s_tq")
        s_tqe = sem("s_tqe")
        s_rot = sem("s_rot")
        s_kd = sem("s_kd")
        s_s = sem("s_s")
        s_mx = sem("s_mx")
        s_exp = sem("s_exp")
        s_pt = sem("s_pt")
        s_pte = sem("s_pte")
        s_pv = sem("s_pv")
        s_yev = sem("s_yev")
        s_st = sem("s_st")
        s_stm = sem("s_stm")
        s_ro = sem("s_ro")
        s_r = sem("s_r")
        s_re = sem("s_re")
        s_qd = sem("s_qd")
        s_rsq = sem("s_rsq")
        s_ssr = sem("s_ssr")
        s_stdr = sem("s_stdr")
        s_yr = sem("s_yr")
        s_wo = sem("s_wo")
        s_xo = sem("s_xo")
        s_h2 = sem("s_h2")
        s_lg = sem("s_lg")
        s_ge = sem("s_ge")
        s_gex = sem("s_gex")
        s_td = sem("s_td")
        s_te = sem("s_te")
        s_sel = sem("s_sel")
        s_cnt = sem("s_cnt")
        s_row = sem("s_row")
        s_tabt = sem("s_tabt")
        s_slot = sem("s_slot")
        s_xgt = sem("s_xgt")
        s_xgh = sem("s_xgh")
        s_xgl = sem("s_xgl")
        s_gu = sem("s_gu")
        s_sil = sem("s_sil")
        s_hid = sem("s_hid")
        s_ht = sem("s_ht")
        s_hth = sem("s_hth")
        s_htl = sem("s_htl")
        s_y = sem("s_y")
        s_ye = sem("s_ye")
        s_yfree = sem("s_yfree")
        s_cmb = sem("s_cmb")
        s_pair = sem("s_pair")
        s_last = sem("s_last")

        block = ctx.enter_context(nc.Block())

        class Chain:
            def __init__(self, eng, s):
                self.eng, self.s, self.n = eng, s, 0

            def __call__(self, ins):
                self.n += 1
                ins.then_inc(self.s, 1)
                self.eng.wait_ge(self.s, self.n)

        def bc(ap, shape):
            return ap.to_broadcast(shape)

        def apart(eng):
            eng.sem_inc(s_apart, 1)

        def make_hi(eng, base, n):
            eng.wait_ge(s_stage[n % NS], base * (16 // NS) + 16 * (n // NS + 1))
            eng.wait_ge(s_used, base + n + 1)
            eng.activation(w_hi[:, n % NW, :], stage[:, n % NS, :], ACT.Copy).then_inc(s_hi, 1)

        def make_lo(eng, base, n):
            eng.wait_ge(s_hi, base + n + 1)
            eng.tensor_tensor(w_lo[:, n % NW, :], stage[:, n % NS, :],
                              w_hi[:, n % NW, :].bitcast(f32), ALU.subtract).then_inc(s_lo, 1)

        def rounds_of(eng):
            return eng.value_load(rounds_i[0:1, 0:1], min_val=1, max_val=NT)

        def meet(eng, p):
            eng.sem_inc(s_arrive, 1)
            eng.wait_ge(s_go, p + 1)

        @block.sync
        def _(sp):
            passes = sp.alloc_register("sp_passes")
            sp.reg_mov(passes, 0)

            def load(base, n, src, split=2):
                sp.wait_ge(s_lo, base + n + 1)
                apart(sp)
                dst = stage[:, n % NS, :].rearrange("p (k c) -> p k c", k=split)
                sp.dma_start(dst, src).then_inc(s_stage[n % NS], 16)

            def tiles(w, row, col):
                return w[row:row + 256, col:col + CH].rearrange("(k p) c -> p k c", p=128)

            def load_pass(base0):
                with sp.Fori(0, E_N // 2) as pair:
                    base = sp.snap(base0 + pair * (2 * U_E))
                    for i in range(2):
                        e = sp.snap(flat[0] + pair * 2 + i)
                        for n in range(2 * FT):
                            w = (a["w_exp_gate"], a["w_exp_up"])[n % 2].rearrange("l e d f -> (l e) d f")
                            src = w[bass.ds(e, 1), (n // 2) * 256:(n // 2 + 1) * 256, :]\
                                .rearrange("o (k p) c -> p (o k) c", p=128)
                            load(base, U_E * i + n, src)
                        w = a["w_exp_down"].rearrange("l e f d -> (l e) f d")
                        for n in range(FT):
                            src = w[bass.ds(e, 1), n * 128:(n + 1) * 128, :].rearrange("o p c -> p o c")
                            load(base, U_E * i + 2 * FT + n, src, split=1)

            flat = [None]
            with sp.Fori(0, DEPTH) as layer:
                p = sp.snap(passes, min_val=0, max_val=NT * DEPTH)
                base = sp.snap(layer * U_ATT + p * U_PASS)

                def of(w, r, c):
                    return w[bass.ds(layer, 1), r:r + 256, c:c + CH].rearrange("o (k p) c -> p (o k) c", p=128)

                for n in range(U_MEM):
                    load(base, n, of(a["w_mem_kv"], 256 * n, 0))
                for q, c in enumerate(CHUNKS):
                    for n in range(4):
                        load(base, U_MEM + 4 * q + n, of(a["w_in"], 256 * n, CH * c))
                for q in range(2):
                    for n in range(4):
                        load(base, U_MEM + U_PROJ + 4 * q + n, of(a["w_out"], 256 * n, CH * q))
                flat[0] = sp.snap(layer * E_N)
                load_pass(sp.snap(layer * U_ATT + U_ATT + p * U_PASS))
                sp.reg_add(passes, passes, 1)
                sp.wait_ge(s_rounds, layer + 1)
                apart(sp)
                rounds = rounds_of(sp)
                with sp.If(rounds > 1):
                    with sp.Fori(1, rounds) as r:
                        p2 = sp.snap(passes, min_val=1, max_val=NT * DEPTH)
                        load_pass(sp.snap(layer * U_ATT + U_ATT + p2 * U_PASS))
                        sp.reg_add(passes, passes, 1)
                with sp.Else():
                    sp.nop()
            for t in range(NT):
                sp.wait_ge(s_x, 16 * DEPTH + 4 * (t + 1))
                sp.dma_start(out[0, t * 128:(t + 1) * 128, :], x[:, t, :]).then_inc(s_out, 16)
            sp.wait_ge(s_out, 16 * NT)

        @block.gpsimd
        def _(pool):
            pool.dma_start(con[:, :], a["const_pack"]).then_inc(s_const, 16)
            pool.dma_start(x[:, :, :], a["x"][0].rearrange("(t p) d -> p t d", p=128)).then_inc(s_xin, 16)
            pool.memset(gp[:, :, :], NEG).then_inc(s_pad, 1)
            pool.memset(ep[:, :, :], NEG).then_inc(s_pad, 1)
            pool.wait_ge(s_const, 16)
            passes = pool.alloc_register("pool_passes")
            pool.reg_mov(passes, 0)
            with pool.Fori(0, DEPTH) as layer:
                chain = Chain(pool, s_pool)

                def row(w):
                    return w[bass.ds(layer, 1), :].rearrange("o n -> (o n)").partition_broadcast(128)

                pool.dma_start(act[:, 2:4, :], a["mem"][0].rearrange("(t p) d -> p t d", p=128)).then_inc(s_memx, 16)
                pool.dma_start(gvec[:, :], row(a["mem_norm_g"])).then_inc(s_gain[0], 16)
                pool.dma_start(g_ret[:, :], row(a["ret_norm_g"].rearrange("l h v -> l (h v)"))).then_inc(s_small, 16)
                for i, name in enumerate(("moba_qn_g", "moba_kn_g", "mem_qn_g", "mem_kn_g")):
                    pool.dma_start(g_head[:, i, :], row(a[name])).then_inc(s_small, 16)
                pool.dma_start(r_bias[:, 0:4], row(a["b_router_grp"])).then_inc(s_small, 16)
                pool.dma_start(r_bias[:, 4:20], row(a["b_router_exp"])).then_inc(s_small, 16)
                for lo_c, hi_c, name in ((0, 4, "w_router_grp"), (4, 20, "w_router_exp")):
                    pool.dma_start(wr[:, :, lo_c:hi_c], a[name][bass.ds(layer, 1), :, :]
                                   .rearrange("o (k p) e -> p (o k) e", p=128)).then_inc(s_wr, 16)
                pool.dma_start(tab_d.rearrange("(n q) o -> n (q o)", q=128), const("empty", 64)).then_inc(s_tabi, 16)
                pool.wait_ge(s_hm, 2)
                pool.dma_start(gvec[:, :], row(a["norm1_g"])).then_inc(s_gain[1], 16)
                pool.wait_ge(s_h1, 4)
                pool.dma_start(gvec[:, :], row(a["norm2_g"])).then_inc(s_gain[2], 16)

                pool.wait_ge(s_pev, 12)
                pool.wait_ge(s_tr, 12)
                for t in range(NT):
                    v = pq[0][:, t, :].rearrange("p (h s c) -> p h s c", h=8, s=2)
                    va = rot_a.rearrange("p (h s c) -> p h s c", h=8, s=2)
                    vb = rot_b.rearrange("p (h s c) -> p h s c", h=8, s=2)
                    v16 = pq[0][:, t, :].rearrange("p (g c) -> p g c", g=16)
                    a16 = rot_a.rearrange("p (g c) -> p g c", g=16)
                    b16 = rot_b.rearrange("p (g c) -> p g c", g=16)
                    chain(pool.tensor_tensor(a16, v16, bc(cos_t[:, t, :].unsqueeze(1), [128, 16, 32]), ALU.mult))
                    chain(pool.tensor_tensor(b16, v16, bc(sin_t[:, t, :].unsqueeze(1), [128, 16, 32]), ALU.mult))
                    chain(pool.tensor_tensor(v[:, :, 0, :], va[:, :, 0, :], vb[:, :, 1, :], ALU.subtract))
                    chain(pool.tensor_tensor(v[:, :, 1, :], vb[:, :, 0, :], va[:, :, 1, :], ALU.add))
                pool.sem_inc(s_rot, 1)
                for t in range(2):
                    pool.tensor_tensor(kd[:, t, :].rearrange("p (h c) -> p h c", h=H),
                                       pq[0][:, t, 256:512].rearrange("p (h c) -> p h c", h=H),
                                       bc(kdec[:, t, :].unsqueeze(2), [128, H, DH]), ALU.mult).then_inc(s_kd, 1)

                for t in range(NT):
                    pool.wait_ge(s_h2, t + 1)
                    pool.dma_start(h2_d[t * 128:(t + 1) * 128, :], act[:, t, :]).then_inc(s_h2st, 16)
                pool.wait_ge(s_tabi, layer * 16 + 16)
                apart(pool)
                pool.wait_ge(s_row, 1)
                for q in range(2):
                    for t in range(NT):
                        pool.indirect_dma_start(
                            out=tab_d, out_offset=bass.IndirectOffsetOnAxis(ap=row_i[:, q, t:t + 1], axis=0),
                            in_=const("pairid")[:, NT * q + t:NT * q + t + 1], in_offset=None).then_inc(s_tabw, 16)
                pool.wait_ge(s_tabw, layer * 128 + 128)
                apart(pool)
                pool.dma_start(tab[:, :], tab_d.rearrange("(n q) o -> n (q o)", q=128)).then_inc(s_tabr, 16)
                pool.wait_ge(s_h2st, layer * 64 + 64)
                apart(pool)
                pool.wait_ge(s_slot, 1)
                pool.wait_ge(s_known, 1)
                rounds = rounds_of(pool)
                with pool.Fori(0, rounds) as r:
                    p = pool.snap(passes, min_val=0, max_val=NT * DEPTH)

                    def gather(i, col):
                        pool.tensor_copy(tok_now[:, i, :], slot_tok[:, bass.ds(col, 1)]).then_inc(s_last, 1)

                    def gather_dma(i):
                        pool.indirect_dma_start(
                            out=xg[:, i, :], out_offset=None, in_=h2_d,
                            in_offset=bass.IndirectOffsetOnAxis(ap=tok_now[:, i, :], axis=0),
                            bounds_check=SEQ - 1, oob_is_err=False).then_inc(s_xg[i], 16)

                    def scatter(i, e2, pair16, col):
                        pool.wait_ge(s_ye, e2 + (i + 2))
                        pool.tensor_copy(pair_now[:, i, :], slot_pair[:, bass.ds(col, 1)]).then_inc(s_pair, 1)
                        pool.wait_ge(s_pair, e2 + (i + 1))
                        apart(pool)
                        pool.indirect_dma_start(
                            out=y_d, out_offset=bass.IndirectOffsetOnAxis(ap=pair_now[:, i, :], axis=0),
                            in_=ysb[:, i, :], in_offset=None,
                            bounds_check=2 * SEQ - 1, oob_is_err=False).then_inc(s_yst[i], 16)
                        pool.wait_ge(s_yst[i], pair16 + 16)
                        pool.sem_inc(s_yfree, 1)

                    pool.sem_inc(s_yfree, 2)
                    for i in range(2):
                        gather(i, r + 4 * i)
                        pool.wait_ge(s_last, i + 1)
                        gather_dma(i)
                    with pool.Fori(0, E_N // 2 - 1) as pair:
                        e2 = pool.snap(pair * 2)
                        for i in range(2):
                            pool.wait_ge(s_xgt, e2 + (i + 1))
                            gather(i, pair * 8 + r + (8 + 4 * i))
                            pool.wait_ge(s_last, e2 + (i + 3))
                            apart(pool)
                            gather_dma(i)
                            scatter(i, e2, p * 128 + pair * 16, pair * 8 + r + 4 * i)
                    for i in range(2):
                        scatter(i, E_N - 2, p * 128 + (8 * E_N - 16), r + 4 * (E_N - 2 + i))
                    pool.wait_ge(s_arrive, p * 3 + 3)
                    apart(pool)
                    pool.sem_clear(range(s_first.num, s_last.num + 1))
                    pool.sem_inc(s_go, 1)
                    pool.reg_add(passes, passes, 1)
                for q in range(2 * NT):
                    if q >= 4:
                        pool.wait_ge(s_cmb, q - 3)
                    r0 = SEQ * (q % 2) + 128 * (q // 2)
                    pool.dma_start(act[:, q % 4, :], y_d[r0:r0 + 128, :]).then_inc(s_yg[q % 4], 16)
                pool.wait_ge(s_cmb, 2 * NT)

        @block.scalar
        def _(sc):
            sc.wait_ge(s_const, 16)
            passes = sc.alloc_register("act_passes")
            sc.reg_mov(passes, 0)
            with sc.Fori(0, DEPTH) as layer:
                p = sc.snap(passes, min_val=0, max_val=NT * DEPTH)
                base = sc.snap(layer * U_ATT + p * U_PASS)
                chain = Chain(sc, s_act)

                def squares(src, col):
                    chain(sc.activation(junk, src, ACT.Square, accum_out=ss[:, col:col + 1]))

                def root(dst, src, n, s):
                    sc.activation(dst, src, ACT.Sqrt, bias=eps, scale=1.0 / n).then_inc(s, 1)

                def bank_hi(j, b, dst):
                    sc.wait_ge(s_tr, j + 1)
                    sc.activation(dst, bank[b][:, :].rearrange("p (k c) -> p k c", k=4), ACT.Copy).then_inc(s_trh, 1)

                for n in range(3):
                    make_hi(sc, base, n)
                sc.wait_ge(s_memx, layer * 16 + 16)
                for t in range(2):
                    squares(act[:, 2 + t, :], t)
                root(rstd[:, 0:2], ss[:, 0:2], D, s_std)
                sc.wait_ge(s_x, layer * 16 + 16)
                for t in range(NT):
                    squares(x[:, t, :], 2 + t)
                root(rstd[:, 2:6], ss[:, 2:6], D, s_std)
                make_hi(sc, base, 3)
                for j in range(4):
                    bank_hi(j, j, mT_hi[:, 4 * (j % 2):4 * (j % 2) + 4, 128 * (j // 2):128 * (j // 2) + 128])
                for k in range(4):
                    make_hi(sc, base, 4 + k)
                    for j in (2 * k, 2 * k + 1):
                        bank_hi(4 + j, (6, 7, 0, 1, 2, 3, 6, 7)[j],
                                hT_hi[:, 4 * (j % 2):4 * (j % 2) + 4, 128 * k:128 * k + 128])
                for t in range(2):
                    sc.wait_ge(s_mkv, 1)
                    sc.activation(ck[:, t, 0:256], bank[4 + t][:, 0:256], ACT.Copy)
                    sc.activation(cv[:, t, :], bank[4 + t][:, 256:512], ACT.Copy).then_inc(s_mkve, 1)
                sc.wait_ge(s_wr, layer * 32 + 32)
                sc.activation(wr_hi[:, :, :], wr[:, :, :], ACT.Copy).then_inc(s_wrh, 1)

                def evacuate(n):
                    for t in range(NT):
                        sc.wait_ge(s_proj, 4 * n + t + 1)
                        sc.activation(pq[CHUNKS[n]][:, t, :], bank[4 * (n % 2) + t][:, :],
                                      ACT.Silu if CHUNKS[n] == 2 else ACT.Copy).then_inc(s_pev, 1)

                for n in range(3):
                    for k in range(4):
                        make_hi(sc, base, 8 + 4 * n + k)
                    if n:
                        sc.wait_ge(s_ssq, n)
                        part_ = slice(0, 32) if n == 1 else slice(32, 56)
                        root(rstdq[:, part_], ssq[:, part_], DH, s_stdq)
                    evacuate(n)
                for j in range(24):
                    t, q = j // 6, j % 6
                    sc.wait_ge(s_mx, j + 1)
                    if j >= 2:
                        sc.wait_ge(s_pt, j - 1)
                    if q < 2:
                        for g in range(2):
                            ins = sc.activation(probs[:, j % 2, 256 * g:256 * g + 256],
                                                bank[j % 2][:, 256 * g:256 * g + 256], ACT.Exp,
                                                bias=nmx[:, j % 2, g:g + 1], scale=DH ** -0.5,
                                                accum_out=rsum[:, t, 4 + q + 2 * g:5 + q + 2 * g])
                    else:
                        w = 128 * (t + 1)
                        ins = sc.activation(probs[:, j % 2, 0:w], bank[j % 2][:, 0:w], ACT.Exp,
                                            bias=nmx[:, j % 2, 0:1], scale=DH ** -0.5,
                                            accum_out=rsum[:, t, q - 2:q - 1])
                    ins.then_inc(s_exp, 1)
                for n in (3, 4):
                    for k in range(4):
                        make_hi(sc, base, 8 + 4 * n + k)
                    evacuate(n)
                for t in range(NT):
                    sc.wait_ge(s_ro, H * (t // 2 + 1))
                    sc.wait_ge(s_stm, 8)
                    if t:
                        sc.wait_ge(s_ssr, t)
                    else:
                        sc.wait_ge(s_ro, 8)
                    sc.activation(sqr, bank[(2, 3, 6, 7)[t]][:, :], ACT.Square).then_inc(s_rsq, 1)
                sc.wait_ge(s_ssr, NT)
                root(rstdr[:, :], ssr[:, :], 128, s_stdr)
                for j in range(8):
                    bank_hi(12 + j, (0, 1, 4, 5)[j % 4],
                            hT_hi[:, 4 * (j % 2):4 * (j % 2) + 4, 128 * (j // 2):128 * (j // 2) + 128])
                for k in range(4):
                    make_hi(sc, base, 28 + k)
                for t in range(NT):
                    sc.wait_ge(s_xo, 5 + t)
                    squares(x[:, t, :], 6 + t)
                root(rstd[:, 6:10], ss[:, 6:10], D, s_std)
                base_m = sc.snap(layer * U_ATT + U_ATT + p * U_PASS)
                for j in range(8):
                    bank_hi(20 + j, (2, 3, 6, 7, 0, 1, 4, 5)[j],
                            hT_hi[:, 4 * (j % 2):4 * (j % 2) + 4, 128 * (j // 2):128 * (j // 2) + 128])
                sc.wait_ge(s_ge, 1)
                sc.activation(gexp[:, :, :], gexp[:, :, :], ACT.Exp).then_inc(s_gex, 1)
                sc.wait_ge(s_td, 1)
                sc.activation(te[:, :], td[:, :], ACT.Exp).then_inc(s_te, 1)

                sc.wait_ge(s_known, 1)
                rounds = rounds_of(sc)
                with sc.Fori(0, rounds) as r:
                    p2 = sc.snap(passes, min_val=0, max_val=NT * DEPTH)
                    base_p = sc.snap(layer * U_ATT + U_ATT + p2 * U_PASS)
                    sc.sem_inc(s_ye, 1)
                    for n in range(3):
                        make_hi(sc, base_p, n)

                    def rows_hi(i, count):
                        sc.wait_ge(s_xgt, count)
                        for q in range(2):
                            ins = sc.activation(xgT_hi[:, i, 4 * q:4 * q + 4, :],
                                                bank[4 + q][:, :].rearrange("p (k c) -> p k c", k=4), ACT.Copy)
                        ins.then_inc(s_xgh, 1)

                    def expert(pair, e2, base_e, i, last=False):
                        n0 = U_E * i
                        for n in range(3, 8):
                            make_hi(sc, base_e, n0 + n)
                        if not last:
                            rows_hi(1 - i, e2 + (i + 2))
                        for n in range(8, 11):
                            make_hi(sc, base_e, n0 + n)
                        sc.wait_ge(s_gu, e2 + (i + 1))
                        sc.activation(sil[:, :], bank[0][:, :], ACT.Silu).then_inc(s_sil, 1)
                        make_hi(sc, base_e, n0 + 11)
                        sc.wait_ge(s_ht, e2 + (i + 1))
                        sc.activation(hidT_hi[:, :, :], bank[7][:, :].rearrange("p (k c) -> p k c", k=4),
                                      ACT.Copy).then_inc(s_hth, 1)
                        if not last:
                            for n in range(3):
                                make_hi(sc, base_e, n0 + U_E + n)
                        sc.wait_ge(s_y, e2 + (i + 1))
                        sc.wait_ge(s_yfree, e2 + (i + 1))
                        for q in range(2):
                            ins = sc.activation(ysb[:, i, 512 * q:512 * q + 512], bank[2 + q][:, :], ACT.Copy)
                        ins.then_inc(s_ye, 1)

                    rows_hi(0, 1)
                    with sc.Fori(0, E_N // 2 - 1) as pair:
                        e2 = sc.snap(pair * 2)
                        base_e = sc.snap(base_p + pair * (2 * U_E))
                        for i in range(2):
                            expert(pair, e2, base_e, i)
                    base_l = sc.snap(base_p + (E_N // 2 - 1) * 2 * U_E)
                    for i in range(2):
                        expert(E_N // 2 - 1, E_N - 2, base_l, i, last=i == 1)
                    sc.wait_ge(s_ye, E_N + 1)
                    meet(sc, p2)
                    sc.reg_add(passes, passes, 1)

        @block.vector
        def _(dv):
            dv.sem_inc(s_lo, NS)
            dv.wait_ge(s_const, 16)
            dv.wait_ge(s_pad, 2)
            dv.wait_ge(s_xin, 16)
            dv.sem_inc(s_x, 16)
            passes = dv.alloc_register("dve_passes")
            dv.reg_mov(passes, 0)
            with dv.Fori(0, DEPTH) as layer:
                p = dv.snap(passes, min_val=0, max_val=NT * DEPTH)
                base = dv.snap(layer * U_ATT + p * U_PASS)
                chain = Chain(dv, s_dve)
                iota = const("iota")

                def bank_lo(j, b, dst, hi):
                    dv.wait_ge(s_trh, j + 1)
                    dv.tensor_tensor(dst, bank[b][:, :].rearrange("p (k c) -> p k c", k=4), hi.bitcast(f32),
                                     ALU.subtract).then_inc(s_trl, 1)

                def hT_part(h, j):
                    return h[:, 4 * (j % 2):4 * (j % 2) + 4, 128 * (j // 2):128 * (j // 2) + 128]

                def norm(dst, src, col, s):
                    dv.scalar_tensor_tensor(out=dst, in0=src, scalar=rstd[:, col:col + 1], in1=gvec[:, :],
                                            op0=ALU.mult, op1=ALU.mult).then_inc(s, 1)

                for n in range(3):
                    make_lo(dv, base, n)
                dv.wait_ge(s_std, 1)
                chain(dv.reciprocal(rstd[:, 0:2], rstd[:, 0:2]))
                dv.wait_ge(s_gain[0], layer * 16 + 16)
                for t in range(2):
                    norm(act[:, 2 + t, :], act[:, 2 + t, :], t, s_hm)
                dv.wait_ge(s_std, 2)
                chain(dv.reciprocal(rstd[:, 2:6], rstd[:, 2:6]))
                make_lo(dv, base, 3)
                for j in range(4):
                    bank_lo(j, j, hT_part(mT_lo, j), hT_part(mT_hi, j))
                dv.wait_ge(s_gain[1], layer * 16 + 16)
                dv.wait_ge(s_tr, 4)
                for t in range(NT):
                    norm(act[:, t, :], x[:, t, :], 2 + t, s_h1)
                for k in range(4):
                    make_lo(dv, base, 4 + k)
                    for j in (2 * k, 2 * k + 1):
                        bank_lo(4 + j, (6, 7, 0, 1, 2, 3, 6, 7)[j], hT_part(hT_lo, j), hT_part(hT_hi, j))
                dv.wait_ge(s_wrh, 1)
                dv.tensor_tensor(wr_lo[:, :, :], wr[:, :, :], wr_hi[:, :, :].bitcast(f32), ALU.subtract)\
                    .then_inc(s_wrl, 1)

                def head_squares(src, heads, dst):
                    v = sq[:, 0:heads * DH]
                    chain(dv.tensor_tensor(v, src, src, ALU.mult))
                    chain(dv.tensor_reduce(dst, v.rearrange("p (h c) -> p h c", h=heads), axis=AX.X, op=ALU.add))

                def head_norm(v, heads, col, gains):
                    v3 = v.rearrange("p (h c) -> p h c", h=heads)
                    chain(dv.tensor_tensor(v3, v3, bc(rstdq[:, col:col + heads].unsqueeze(2), [128, heads, DH]),
                                           ALU.mult))
                    n = heads // len(gains)
                    for q, g in enumerate(gains):
                        part_ = v3[:, q * n:(q + 1) * n, :]
                        chain(dv.tensor_tensor(part_, part_, bc(g_head[:, g, :].unsqueeze(1), [128, n, DH]), ALU.mult))

                def heads_out(j, b, dst):
                    dv.wait_ge(s_tq, j + 1)
                    dv.tensor_copy(dst, bank[b][:, :]).then_inc(s_tqe, 1)

                dv.wait_ge(s_small, layer * 112 + 112)
                for n in range(3):
                    for k in range(4):
                        make_lo(dv, base, 8 + 4 * n + k)
                    if n == 0:
                        for t in range(NT):
                            dv.wait_ge(s_pev, t + 1)
                            head_squares(pq[3][:, t, :], 8, ssq[:, 8 * t:8 * t + 8])
                        dv.sem_inc(s_ssq, 1)
                    if n == 1:
                        dv.wait_ge(s_mkve, 2)
                        for t in range(2):
                            head_squares(ck[:, t, 0:256], 4, ssq[:, 48 + 4 * t:52 + 4 * t])
                        for t in range(NT):
                            dv.wait_ge(s_pev, 4 + t + 1)
                            head_squares(pq[4][:, t, 256:512], 4, ssq[:, 32 + 4 * t:36 + 4 * t])
                        dv.sem_inc(s_ssq, 1)
                        dv.wait_ge(s_stdq, 1)
                        chain(dv.reciprocal(rstdq[:, 0:32], rstdq[:, 0:32]))
                        for t in range(NT):
                            head_norm(pq[3][:, t, :], 8, 8 * t, (0, 1))
                    if n == 2:
                        dv.wait_ge(s_stdq, 2)
                        chain(dv.reciprocal(rstdq[:, 32:56], rstdq[:, 32:56]))
                        for t in range(2):
                            head_norm(ck[:, t, 0:256], 4, 48 + 4 * t, (3,))
                        for t in range(NT):
                            head_norm(pq[4][:, t, 256:512], 4, 32 + 4 * t, (2,))
                        dv.sem_inc(s_qn, 1)
                heads_out(0, 4, ckT[:, :, :].rearrange("p g c -> p (g c)"))
                for j in range(1, 7):
                    heads_out(j, 4 + j % 4, hd[:, (j - 1) // 2, (j - 1) % 2, :])

                def probs_out(j):
                    dv.wait_ge(s_pt, j + 1)
                    if j >= 2:
                        dv.wait_ge(s_pv, j - 1)
                    w = 512 if j % 6 < 2 else 128 * (j // 6 + 1)
                    dv.tensor_copy(probsT[:, j % 2, 0:w], bank[2 + j % 2][:, 0:w]).then_inc(s_pte, 1)

                def tile_out(t):
                    dv.wait_ge(s_pv, 6 * t + 6)
                    chain(dv.reciprocal(rinv[:, t, :], rsum[:, t, :]))
                    dv.tensor_tensor(act[:, t, 512:1024].rearrange("p (h c) -> p h c", h=8),
                                     bank[4 + t % 2][:, :].rearrange("p (h c) -> p h c", h=8),
                                     bc(rinv[:, t, :].unsqueeze(2), [128, 8, DH]), ALU.mult).then_inc(s_yev, 1)

                for j in range(24):
                    t, q = j // 6, j % 6
                    dv.wait_ge(s_s, j + 1)
                    if j >= 2:
                        dv.wait_ge(s_exp, j - 1)
                    if q < 2:
                        chain(dv.tensor_reduce(mx[:, 0:2], bank[j % 2][:, :].rearrange("p (g c) -> p g c", g=2),
                                               axis=AX.X, op=ALU.max))
                        dv.tensor_scalar(nmx[:, j % 2, :], mx[:, 0:2], -DH ** -0.5, None, ALU.mult).then_inc(s_mx, 1)
                    else:
                        own = bank[j % 2][:, 128 * t:128 * t + 128]
                        chain(dv.tensor_tensor(own, own, const("causal"), ALU.add))
                        chain(dv.tensor_reduce(mx[:, 0:1], bank[j % 2][:, 0:128 * (t + 1)], axis=AX.X, op=ALU.max))
                        dv.tensor_scalar(nmx[:, j % 2, 0:1], mx[:, 0:1], -DH ** -0.5, None, ALU.mult)\
                            .then_inc(s_mx, 1)
                    dv.wait_ge(s_mx, j + 1)
                    if j >= 1:
                        probs_out(j - 1)
                    if j >= 7 and j % 6 == 1:
                        tile_out(j // 6 - 1)
                probs_out(23)
                tile_out(3)

                for n in (3, 4):
                    for k in range(4):
                        make_lo(dv, base, 8 + 4 * n + k)
                for j in range(4):
                    heads_out(7 + j, 4 + j, hd[:, j // 2, j % 2, :])
                dv.wait_ge(s_tqe, 11)
                chain(dv.memset(state, 0.0))
                dv.tensor_tensor(qdT, hd[:, 0, :, 256:512], qdec, ALU.mult).then_inc(s_qd, 1)
                for r in range(8):
                    h = r % 4
                    dv.wait_ge(s_st, r + 1)
                    if r >= 2:
                        dv.wait_ge(s_ro, r - 1)
                    dv.tensor_tensor(probs[:, r % 2, 0:256], bank[r % 2][:, 0:256], dmask[:, h, :], ALU.mult)
                    dv.tensor_tensor(probs[:, r % 2, 256:384], bank[r % 2][:, 256:384], dmask[:, h, 0:128],
                                     ALU.mult).then_inc(s_stm, 1)
                    if r == 2:
                        dv.wait_ge(s_r, 1)
                        for g in range(2):
                            half = slice(64 * g, 64 * g + 64)
                            ins = dv.tensor_copy(state[half, :, 128 * g:128 * g + 128],
                                                 bank[4][half, 0:256].rearrange("p (g c) -> p g c", g=2))
                        ins.then_inc(s_re, 1)
                for t in range(NT):
                    dv.wait_ge(s_rsq, t + 1)
                    dv.tensor_reduce(ssr[:, 4 * t:4 * t + 4], sqr.rearrange("p (h c) -> p h c", h=H), axis=AX.X,
                                     op=ALU.add).then_inc(s_ssr, 1)
                dv.wait_ge(s_stdr, 1)
                chain(dv.reciprocal(rstdr[:, :], rstdr[:, :]))
                dv.wait_ge(s_rot, 1)
                dv.wait_ge(s_pev, 20)
                for t in range(NT):
                    y3 = act[:, t, 0:512].rearrange("p (h c) -> p h c", h=H)
                    chain(dv.tensor_tensor(y3, bank[(2, 3, 6, 7)[t]][:, :].rearrange("p (h c) -> p h c", h=H),
                                           bc(rstdr[:, 4 * t:4 * t + 4].unsqueeze(2), [128, H, 128]), ALU.mult))
                    chain(dv.tensor_tensor(act[:, t, 0:512], act[:, t, 0:512], g_ret[:, :], ALU.mult))
                    dv.tensor_tensor(act[:, t, 0:512], act[:, t, 0:512], pq[2][:, t, :], ALU.mult).then_inc(s_yr, 1)
                for j in range(8):
                    bank_lo(12 + j, (0, 1, 4, 5)[j % 4], hT_part(hT_lo, j), hT_part(hT_hi, j))
                for k in range(4):
                    make_lo(dv, base, 28 + k)
                for n in range(2):
                    for t in range(NT):
                        dv.wait_ge(s_wo, 4 * n + t + 1)
                        v = x[:, t, 512 * n:512 * n + 512]
                        dv.tensor_tensor(v, bank[((2, 3, 6, 7), (0, 1, 4, 5))[n][t]][:, :], v, ALU.add)\
                            .then_inc(s_xo, 1)
                dv.wait_ge(s_std, 3)
                chain(dv.reciprocal(rstd[:, 6:10], rstd[:, 6:10]))
                dv.wait_ge(s_gain[2], layer * 16 + 16)
                dv.wait_ge(s_tr, 20)
                for t in range(NT):
                    norm(act[:, t, :], x[:, t, :], 6 + t, s_h2)
                for j in range(8):
                    bank_lo(20 + j, (2, 3, 6, 7, 0, 1, 4, 5)[j], hT_part(hT_lo, j), hT_part(hT_hi, j))
                dv.wait_ge(s_lg, 1)
                chain(dv.tensor_tensor(lg[:, :, :], bank[2][:, 0:80].rearrange("p (t c) -> p t c", t=NT),
                                       bc(r_bias[:, :].unsqueeze(1), [128, NT, 20]), ALU.add))
                chain(dv.tensor_copy(gp[:, :, 0:4], lg[:, :, 0:4]))
                for t in range(NT):
                    ins = dv.max(top[:, t, :], gp[:, t, :])
                chain(ins)
                for t in range(NT):
                    ins = dv.max_index(topi[:, t, :], top[:, t, :], gp[:, t, :])
                dv.tensor_tensor(gexp[:, :, :], gp[:, :, 0:4], bc(top[:, :, 0:1], [128, NT, 4]), ALU.subtract)\
                    .then_inc(s_ge, 1)
                dv.wait_ge(s_ge, 1)
                chain(dv.tensor_copy(gnum[:, :], topi[:, :, 0]))
                chain(dv.tensor_tensor(oneg[:, :, :], bc(iota[:, 0:4].unsqueeze(1), [128, NT, 4]),
                                       bc(gnum[:, :].unsqueeze(2), [128, NT, 4]), ALU.is_equal))
                p4 = prod[:, :, :].rearrange("p t (g j) -> p t g j", g=4)
                chain(dv.tensor_tensor(p4, lg[:, :, 4:20].rearrange("p t (g j) -> p t g j", g=4),
                                       bc(oneg[:, :, :].unsqueeze(3), [128, NT, 4, 4]), ALU.mult))
                chain(dv.tensor_reduce(ep[:, :, 0:4], prod[:, :, :].rearrange("p t (g j) -> p t j g", g=4),
                                       axis=AX.X, op=ALU.add))
                for t in range(NT):
                    ins = dv.max(top[:, t, :], ep[:, t, :])
                chain(ins)
                dv.tensor_tensor(td[:, :], top[:, :, 1], top[:, :, 0], ALU.subtract).then_inc(s_td, 1)
                for t in range(NT):
                    ins = dv.max_index(topi[:, t, :], top[:, t, :], ep[:, t, :])
                chain(ins)
                for q in range(2):
                    chain(dv.tensor_copy(enum[:, q, :], topi[:, :, q]))
                    chain(dv.scalar_tensor_tensor(out=enum[:, q, :], in0=gnum[:, :], scalar=4.0, in1=enum[:, q, :],
                                                  op0=ALU.mult, op1=ALU.add))
                    chain(dv.tensor_tensor(one_e[:, q, :, :], bc(iota.unsqueeze(1), [128, NT, 16]),
                                           bc(enum[:, q, :].unsqueeze(2), [128, NT, 16]), ALU.is_equal))
                dv.tensor_tensor(sel[:, :, :], one_e[:, 0, :, :], one_e[:, 1, :, :], ALU.add).then_inc(s_sel, 1)
                dv.wait_ge(s_gex, 1)
                chain(dv.tensor_reduce(gw[:, :], gexp[:, :, :], axis=AX.X, op=ALU.add))
                chain(dv.reciprocal(gw[:, :], gw[:, :]))
                dv.wait_ge(s_te, 1)
                chain(dv.tensor_scalar(td[:, :], te[:, :], 1.0, None, ALU.add))
                chain(dv.reciprocal(td[:, :], td[:, :]))
                chain(dv.tensor_tensor(wtok[:, 0, :], td[:, :], gw[:, :], ALU.mult))
                chain(dv.tensor_tensor(wtok[:, 1, :], wtok[:, 0, :], te[:, :], ALU.mult))
                dv.wait_ge(s_cnt, 1)
                before = bank[3][:, 0:64].rearrange("p (t c) -> p t c", t=NT)
                for q in range(2):
                    chain(dv.tensor_tensor(prod[:, :, :], before, one_e[:, q, :, :], ALU.mult))
                    chain(dv.tensor_reduce(pos[:, q, :], prod[:, :, :], axis=AX.X, op=ALU.add))
                    chain(dv.scalar_tensor_tensor(out=pos[:, q, :], in0=enum[:, q, :], scalar=float(SEQ),
                                                  in1=pos[:, q, :], op0=ALU.mult, op1=ALU.add))
                dv.tensor_copy(row_i[:, :, :], pos[:, :, :]).then_inc(s_row, 1)
                chain(dv.tensor_reduce(tmpr[:, 0:1], bank[3][:, 64:80], axis=AX.X, op=ALU.max))
                chain(dv.tensor_scalar(tmpr[:, 1:4], const("limits"), tmpr[:, 0:1], None, ALU.is_lt))
                chain(dv.tensor_reduce(tmpr[:, 0:1], tmpr[:, 1:4], axis=AX.X, op=ALU.add))
                dv.tensor_scalar(rounds_i[:, :], tmpr[:, 0:1], 1.0, None, ALU.add).then_inc(s_known, 1)
                dv.wait_ge(s_known, 1)
                dv.sem_inc(s_rounds, 1)
                dv.wait_ge(s_tabt, 1)
                chain(dv.tensor_copy(pair_f[:, :], bank[6][:, 0:64]))
                dv.tensor_copy(slot_pair[:, :], pair_f[:, :])
                chain(dv.tensor_scalar(tok_f[:, :], pair_f[:, :], float(SEQ), -float(SEQ), ALU.is_ge, ALU.mult))
                dv.tensor_tensor(slot_tok[:, :], tok_f[:, :], pair_f[:, :], ALU.add).then_inc(s_slot, 1)

                dv.wait_ge(s_known, 1)
                rounds = rounds_of(dv)
                with dv.Fori(0, rounds) as r:
                    p2 = dv.snap(passes, min_val=0, max_val=NT * DEPTH)
                    base_p = dv.snap(layer * U_ATT + U_ATT + p2 * U_PASS)
                    for n in range(3):
                        make_lo(dv, base_p, n)

                    def rows_lo(i, count):
                        dv.wait_ge(s_xgh, count)
                        for q in range(2):
                            ins = dv.tensor_tensor(xgT_lo[:, i, 4 * q:4 * q + 4, :],
                                                   bank[4 + q][:, :].rearrange("p (k c) -> p k c", k=4),
                                                   xgT_hi[:, i, 4 * q:4 * q + 4, :].bitcast(f32), ALU.subtract)
                        ins.then_inc(s_xgl, 1)

                    def expert(e2, base_e, i, last=False):
                        n0 = U_E * i
                        for n in range(3, 8):
                            make_lo(dv, base_e, n0 + n)
                        if not last:
                            rows_lo(1 - i, e2 + (i + 2))
                        for n in range(8, 11):
                            make_lo(dv, base_e, n0 + n)
                        dv.wait_ge(s_sil, e2 + (i + 1))
                        dv.tensor_tensor(hid[:, :], bank[1][:, :], sil[:, :], ALU.mult).then_inc(s_hid, 1)
                        make_lo(dv, base_e, n0 + 11)
                        dv.wait_ge(s_hth, e2 + (i + 1))
                        dv.tensor_tensor(hidT_lo[:, :, :], bank[7][:, :].rearrange("p (k c) -> p k c", k=4),
                                         hidT_hi[:, :, :].bitcast(f32), ALU.subtract).then_inc(s_htl, 1)
                        if not last:
                            for n in range(3):
                                make_lo(dv, base_e, n0 + U_E + n)

                    rows_lo(0, 1)
                    with dv.Fori(0, E_N // 2 - 1) as pair:
                        e2 = dv.snap(pair * 2)
                        base_e = dv.snap(base_p + pair * (2 * U_E))
                        for i in range(2):
                            expert(e2, base_e, i)
                    base_l = dv.snap(base_p + (E_N // 2 - 1) * 2 * U_E)
                    for i in range(2):
                        expert(E_N - 2, base_l, i, last=i == 1)
                    dv.wait_ge(s_htl, E_N)
                    meet(dv, p2)
                    dv.reg_add(passes, passes, 1)
                for q in range(2 * NT):
                    t = q // 2
                    dv.wait_ge(s_yg[q % 4], layer * 32 + 16 * (q // 4 + 1))
                    dv.scalar_tensor_tensor(out=x[:, t, :], in0=act[:, q % 4, :], scalar=wtok[:, q % 2, t:t + 1],
                                            in1=x[:, t, :], op0=ALU.mult, op1=ALU.add).then_inc(s_cmb, 1)
                    dv.wait_ge(s_cmb, q + 1)
                    if q % 2:
                        dv.sem_inc(s_x, 4)

        @block.tensor
        def _(pe):
            pe.sem_inc(s_used, NW)
            pe.wait_ge(s_const, 16)
            passes = pe.alloc_register("pe_passes")
            pe.reg_mov(passes, 0)

            def three(dst, l_hi, l_lo, r_hi, r_lo, start, stop):
                pe.matmul(dst, l_hi, r_hi, start=start, stop=False)
                pe.matmul(dst, l_hi, r_lo, start=False, stop=False)
                return pe.matmul(dst, l_lo, r_hi, start=False, stop=stop)

            def rows(src_hi, src_lo, base, n, j, banks, done=None):
                pe.wait_ge(s_lo, base + n + 1 + NS)
                for t, b in enumerate(banks):
                    for kk in range(2):
                        k = 2 * j + kk
                        ins = three(bank[b][:, :], src_hi[:, k, 128 * t:128 * t + 128],
                                    src_lo[:, k, 128 * t:128 * t + 128],
                                    w_hi[:, n % NW, 512 * kk:512 * kk + 512], w_lo[:, n % NW, 512 * kk:512 * kk + 512],
                                    start=k == 0, stop=k == KT - 1)
                    if j == 3 and done is not None and t < len(banks) - 1:
                        ins.then_inc(done, 1)
                ins.then_inc(s_used, 1)
                if j == 3 and done is not None:
                    pe.wait_ge(s_used, base + n + 1 + NW)
                    pe.sem_inc(done, 1)

            def turn(src, b, s, cols=4):
                for q in range(cols):
                    ins = pe.transpose(bank[b][:, 128 * q:128 * q + 128], src(q), ident)
                ins.then_inc(s, 1)

            with pe.Fori(0, DEPTH) as layer:
                p = pe.snap(passes, min_val=0, max_val=NT * DEPTH)
                base = pe.snap(layer * U_ATT + p * U_PASS)
                for j in range(4):
                    pe.wait_ge(s_hm, j // 2 + 1)
                    turn(lambda q: act[:, 2 + j // 2, 512 * (j % 2) + 128 * q:512 * (j % 2) + 128 * q + 128], j, s_tr)
                pe.wait_ge(s_trl, 4)
                for k in range(4):
                    rows(mT_hi, mT_lo, base, k, k, (4, 5))
                    if k == 3:
                        pe.wait_ge(s_used, base + k + 1 + NW)
                        pe.sem_inc(s_mkv, 1)
                    pe.wait_ge(s_h1, k + 1)
                    for j in (2 * k, 2 * k + 1):
                        if j >= 6:
                            pe.wait_ge(s_trl, 4 + j - 5)
                        turn(lambda q: act[:, k, 512 * (j % 2) + 128 * q:512 * (j % 2) + 128 * q + 128],
                             (6, 7, 0, 1, 2, 3, 6, 7)[j], s_tr)
                pe.wait_ge(s_trl, 12)

                def project(n):
                    if n == 1:
                        pe.wait_ge(s_mkve, 2)
                    if n >= 2:
                        pe.wait_ge(s_pev, 4 * (n - 1))
                    for j in range(4):
                        rows(hT_hi, hT_lo, base, 4 + 4 * n + j, j, tuple(range(4 * (n % 2), 4 * (n % 2) + 4)),
                             s_proj)

                for n in range(3):
                    project(n)
                pe.wait_ge(s_qn, 1)
                pe.wait_ge(s_pev, 8)
                for g in range(2):
                    for t in range(2):
                        ins = pe.transpose(bank[4][:, 256 * g + 128 * t:256 * g + 128 * t + 128],
                                           ck[:, t, 128 * g:128 * g + 128], ident)
                ins.then_inc(s_tq, 1)
                for j in range(1, 7):
                    src, off = ((pq[4], 256), (pq[3], 0), (pq[3], 256))[(j - 1) // 2]
                    if j >= 4:
                        pe.wait_ge(s_tqe, j - 3)
                    turn(lambda q: src[:, q, off + 128 * ((j - 1) % 2):off + 128 * ((j - 1) % 2) + 128],
                         4 + j % 4, s_tq)
                pe.wait_ge(s_tqe, 7)
                pe.wait_ge(s_pev, 12)

                def scores(j):
                    t, q = j // 6, j % 6
                    if j >= 2:
                        pe.wait_ge(s_exp, j - 1)
                    tok = slice(128 * t, 128 * t + 128)
                    if q < 2:
                        for g in range(2):
                            part_ = slice(64 * q, 64 * q + 64)
                            ins = pe.matmul(bank[j % 2][:, 256 * g:256 * g + 256], hd[part_, 0, g, tok],
                                            ckT[part_, g, :], start=True, stop=True)
                    else:
                        h = q - 2
                        part_ = slice(64 * (h % 2), 64 * (h % 2) + 64)
                        ins = pe.matmul(bank[j % 2][:, 0:128 * (t + 1)], hd[part_, 1, h // 2, tok],
                                        hd[part_, 2, h // 2, 0:128 * (t + 1)], start=True, stop=True)
                    ins.then_inc(s_s, 1)

                def turn_probs(j):
                    pe.wait_ge(s_exp, j + 1)
                    if j >= 2:
                        pe.wait_ge(s_pte, j - 1)
                    turn(lambda q: probs[:, j % 2, 128 * q:128 * q + 128], 2 + j % 2, s_pt,
                         cols=4 if j % 6 < 2 else j // 6 + 1)

                def values(j):
                    t, q = j // 6, j % 6
                    pe.wait_ge(s_pte, j + 1)
                    if q == 0 and t >= 2:
                        pe.wait_ge(s_yev, t - 1)
                    o = bank[4 + t % 2]
                    if q < 2:
                        for g in range(2):
                            h = q + 2 * g
                            for k in range(2):
                                ins = pe.matmul(o[:, 256 + 64 * h:320 + 64 * h],
                                                probsT[:, j % 2, 256 * g + 128 * k:256 * g + 128 * k + 128],
                                                cv[:, k, 64 * h:64 * h + 64], start=k == 0, stop=k == 1)
                    else:
                        h = q - 2
                        for k in range(t + 1):
                            ins = pe.matmul(o[:, 64 * h:64 * h + 64], probsT[:, j % 2, 128 * k:128 * k + 128],
                                            pq[4][:, k, 64 * h:64 * h + 64], start=k == 0, stop=k == t)
                    ins.then_inc(s_pv, 1)

                for s in range(26):
                    if s < 24:
                        scores(s)
                    if 1 <= s <= 24:
                        turn_probs(s - 1)
                    if s >= 2:
                        values(s - 2)
                pe.wait_ge(s_yev, 4)
                for n in (3, 4):
                    project(n)
                pe.wait_ge(s_rot, 1)
                pe.wait_ge(s_pev, 16)
                for j in range(4):
                    turn(lambda q: pq[0][:, q, 128 * j:128 * j + 128], 4 + j, s_tq)
                pe.wait_ge(s_kd, 2)
                pe.wait_ge(s_tqe, 8)
                for h in range(H):
                    half = slice(64 * (h % 2), 64 * (h % 2) + 64)
                    for t in range(2):
                        ins = pe.matmul(bank[4][half, 128 * (h // 2):128 * (h // 2) + 128],
                                        kd[:, t, 64 * h:64 * h + 64], pq[1][:, t, 128 * h:128 * h + 128],
                                        start=t == 0, stop=t == 1)
                ins.then_inc(s_r, 1)
                pe.wait_ge(s_tqe, 11)
                pe.wait_ge(s_pev, 20)

                def ret_scores(r):
                    c, h = r // 4, r % 4
                    half = slice(64 * (h % 2), 64 * (h % 2) + 64)
                    if r >= 2:
                        pe.wait_ge(s_stm, r - 1)
                    pe.matmul(bank[r % 2][:, 0:256], hd[half, 1, h // 2, 256 * c:256 * c + 128],
                              hd[half, 0, h // 2, 256 * c:256 * c + 256], start=True, stop=True)
                    pe.matmul(bank[r % 2][:, 256:384], hd[half, 1, h // 2, 256 * c + 128:256 * c + 256],
                              hd[half, 0, h // 2, 256 * c + 128:256 * c + 256], start=True, stop=True)\
                        .then_inc(s_st, 1)

                def ret_values(r):
                    c, h = r // 4, r % 4
                    pe.wait_ge(s_stm, r + 1)
                    if r == 4:
                        pe.wait_ge(s_re, 1)
                        pe.wait_ge(s_qd, 1)
                    for tt in range(2):
                        t = 2 * c + tt
                        o = bank[(2, 3, 6, 7)[t]][:, 128 * h:128 * h + 128]
                        parts = [(probs[:, r % 2, 128 * tt:128 * tt + 128], pq[1][:, 2 * c, 128 * h:128 * h + 128])]
                        if tt:
                            parts.append((probs[:, r % 2, 256:384], pq[1][:, 2 * c + 1, 128 * h:128 * h + 128]))
                        if c:
                            parts.append((qdT[:, h // 2, 128 * tt:128 * tt + 128],
                                          state[:, h // 2, 128 * (h % 2):128 * (h % 2) + 128]))
                        for q, (l, rr) in enumerate(parts):
                            ins = pe.matmul(o, l, rr, start=q == 0, stop=q == len(parts) - 1)
                    ins.then_inc(s_ro, 1)

                for r in range(9):
                    if r < 8:
                        ret_scores(r)
                    if r >= 1:
                        ret_values(r - 1)
                for j in range(8):
                    t = j // 2
                    pe.wait_ge(s_yr, t + 1)
                    if j >= 4:
                        pe.wait_ge(s_trl, 12 + j - 3)
                    turn(lambda q: act[:, t, 512 * (j % 2) + 128 * q:512 * (j % 2) + 128 * q + 128],
                         (0, 1, 4, 5)[j % 4], s_tr)
                pe.wait_ge(s_trl, 20)
                for n in range(2):
                    for j in range(4):
                        rows(hT_hi, hT_lo, base, 24 + 4 * n + j, j, ((2, 3, 6, 7), (0, 1, 4, 5))[n], s_wo)
                for j in range(8):
                    pe.wait_ge(s_h2, j // 2 + 1)
                    turn(lambda q: act[:, j // 2, 512 * (j % 2) + 128 * q:512 * (j % 2) + 128 * q + 128],
                         (2, 3, 6, 7, 0, 1, 4, 5)[j], s_tr)
                pe.wait_ge(s_trl, 28)
                pe.wait_ge(s_wrl, 1)
                for t in range(NT):
                    for k in range(KT):
                        ins = three(bank[2][:, 20 * t:20 * t + 20], hT_hi[:, k, 128 * t:128 * t + 128],
                                    hT_lo[:, k, 128 * t:128 * t + 128], wr_hi[:, k, :], wr_lo[:, k, :],
                                    start=k == 0, stop=k == KT - 1)
                ins.then_inc(s_lg, 1)
                pe.wait_ge(s_sel, 1)
                for t in range(NT):
                    for j in range(t + 1):
                        pe.matmul(bank[3][:, 16 * t:16 * t + 16], const("below") if j == t else const("ones"),
                                  sel[:, j, :], start=j == 0, stop=j == t)
                for j in range(NT):
                    ins = pe.matmul(bank[3][:, 64:80], const("ones"), sel[:, j, :], start=j == 0, stop=j == NT - 1)
                ins.then_inc(s_cnt, 1)
                pe.wait_ge(s_tabr, layer * 16 + 16)
                apart(pe)
                pe.transpose(bank[6][:, 0:64], tab[:, :], ident[0:64, 0:64]).then_inc(s_tabt, 1)

                pe.wait_ge(s_known, 1)
                rounds = rounds_of(pe)
                with pe.Fori(0, rounds) as r:
                    p2 = pe.snap(passes, min_val=0, max_val=NT * DEPTH)
                    base_p = pe.snap(layer * U_ATT + U_ATT + p2 * U_PASS)

                    def turn_rows(i, loaded):
                        pe.wait_ge(s_xg[i], loaded)
                        for k in range(KT):
                            ins = pe.transpose(bank[4 + k // 4][:, 128 * (k % 4):128 * (k % 4) + 128],
                                               xg[:, i, 128 * k:128 * k + 128], ident)
                        ins.then_inc(s_xgt, 1)

                    def expert(pair, e2, base_e, i, last=False):
                        pe.wait_ge(s_xgl, e2 + (i + 1))
                        for n in range(8):
                            m = U_E * i + n
                            pe.wait_ge(s_lo, base_e + (m + 1 + NS))
                            for kk in range(2):
                                k = 2 * (n // 2) + kk
                                ins = three(bank[n % 2][:, :], xgT_hi[:, i, k, :], xgT_lo[:, i, k, :],
                                            w_hi[:, m % NW, 512 * kk:512 * kk + 512],
                                            w_lo[:, m % NW, 512 * kk:512 * kk + 512], start=k == 0, stop=k == KT - 1)
                            ins.then_inc(s_used, 1)
                            if n == 3 and not last:
                                turn_rows(1 - i, p2 * 128 + pair * 16 + 16 * (i + 1))
                        pe.wait_ge(s_used, base_e + (U_E * i + 8 + NW))
                        pe.sem_inc(s_gu, 1)
                        pe.wait_ge(s_hid, e2 + (i + 1))
                        for q in range(FT):
                            ins = pe.transpose(bank[7][:, 128 * q:128 * q + 128], hid[:, 128 * q:128 * q + 128], ident)
                        ins.then_inc(s_ht, 1)
                        pe.wait_ge(s_htl, e2 + (i + 1))
                        pe.wait_ge(s_ye, e2 + (i + 1))
                        for k in range(FT):
                            m = U_E * i + 8 + k
                            pe.wait_ge(s_lo, base_e + (m + 1 + NS))
                            for q in range(2):
                                ins = three(bank[2 + q][:, :], hidT_hi[:, k, :], hidT_lo[:, k, :],
                                            w_hi[:, m % NW, 512 * q:512 * q + 512],
                                            w_lo[:, m % NW, 512 * q:512 * q + 512], start=k == 0, stop=k == FT - 1)
                            ins.then_inc(s_used, 1)
                        pe.wait_ge(s_used, base_e + (U_E * i + U_E + NW))
                        pe.sem_inc(s_y, 1)

                    turn_rows(0, p2 * 128 + 16)
                    with pe.Fori(0, E_N // 2 - 1) as pair:
                        e2 = pe.snap(pair * 2)
                        base_e = pe.snap(base_p + pair * (2 * U_E))
                        for i in range(2):
                            expert(pair, e2, base_e, i)
                    base_l = pe.snap(base_p + (E_N // 2 - 1) * 2 * U_E)
                    for i in range(2):
                        expert(E_N // 2 - 1, E_N - 2, base_l, i, last=i == 1)
                    meet(pe, p2)
                    pe.reg_add(passes, passes, 1)


_INS = ["x", "mem", "norm1_g", "w_in", "ret_norm_g", "moba_qn_g", "moba_kn_g", "mem_norm_g", "w_mem_kv", "mem_qn_g",
        "mem_kn_g", "w_out", "norm2_g", "w_router_grp", "b_router_grp", "w_router_exp", "b_router_exp", "w_exp_gate",
        "w_exp_up", "w_exp_down"]


def _constants():
    import numpy as np
    c = np.zeros((128, N_CONST), np.float32)

    def put(name, v):
        v = np.asarray(v, np.float32)
        c[:v.shape[0], OFF[name]:OFF[name] + CONST[name]] = v.reshape(v.shape[0], -1)

    f = np.float32
    p = np.arange(128)
    put("ident", np.eye(128))
    inv = (f(1.0) / (f(10000.0) ** np.linspace(0, 1, 32, dtype=f))).astype(f)
    ang = (np.arange(SEQ, dtype=f)[:, None] * inv[None, :]).astype(f)
    for name, fn in (("cos", np.cos), ("sin", np.sin)):
        put(name, fn(ang).astype(f).reshape(NT, 128, 32).transpose(1, 0, 2))
    log_g = np.log1p(-(f(2.0) ** (f(-5.0) - np.arange(H, dtype=f)))).astype(f)
    n = np.arange(256, dtype=f)
    k_scale = f(DH ** -0.5)
    diff = n[None, :] - p[:, None].astype(f)
    put("dmask", np.stack([np.where(diff >= 0, np.exp(log_g[h] * np.maximum(diff, f(0))), 0) * k_scale
                           for h in range(H)], 1))
    q_decay = np.exp(log_g[:, None] * (n + f(1)))
    put("qdec", np.stack([np.repeat(q_decay[2 * g:2 * g + 2], 64, 0) for g in range(2)], 1))
    k_decay = np.exp(log_g[:, None] * (f(255) - n)) * k_scale
    put("kdec", k_decay.reshape(H, 2, 128).transpose(2, 1, 0))
    put("causal", np.where(p[None, :] <= p[:, None], 0.0, NEG))
    put("below", p[:, None] < p[None, :])
    put("ones", np.ones((128, 128)))
    put("iota", np.tile(np.arange(16), (128, 1)))
    put("pairid", p[:, None] + 128 * np.arange(2 * NT)[None, :])
    put("empty", np.full((64, 128), EMPTY))
    put("limits", np.tile(128 * np.arange(1, NT), (128, 1)))
    put("eps", np.full((128, 1), 1e-6))
    return c


def kernel(**inputs):
    import numpy as _np
    import concourse.bacc as _bacc
    from concourse import mybir as _mybir
    from concourse.bass_utils import run_bass_kernel_spmd as _run

    nc = _bacc.Bacc("TRN2", target_bir_lowering=False, num_devices=1)
    arrays, args = {}, {}
    given = {name: _np.ascontiguousarray(inputs[name]) for name in _INS}
    given["const_pack"] = _constants()
    for name, arr in given.items():
        arrays[f"in_{name}"] = arr
        args[name] = nc.dram_tensor(f"in_{name}", arr.shape, _mybir.dt.from_np(arr.dtype), kind="ExternalInput").ap()
    out = nc.dram_tensor("out_x", (1, SEQ, D), _mybir.dt.float32, kind="ExternalOutput").ap()
    build(nc, args, out)
    r = _run(nc, [arrays], core_ids=[0])
    return r.results[0]["out_x"]
```

```python
import concourse.bass as bass
from concourse import mybir
from contextlib import ExitStack

DEPTH, SEQ, D, MEM = 2, 512, 1024, 256
D_IN, E_N, FF = 2560, 16, 512
NT = SEQ // 128
KT = D // 128
FT = FF // 128
H, DH = 4, 64
CH = 512
NS, NW = 8, 4
U_MEM, U_PROJ, U_OUT = 4, 20, 8
U_ATT = U_MEM + U_PROJ + U_OUT
U_E = 12
U_PASS = U_E * E_N
U_FIRST = 8
PAIRS = (E_N - 2) // 2
TURN_E = 3
EARLY = range(U_FIRST + 3, U_FIRST + 3 + 8)
CHUNK_BANK = [0, 4, 0, 4, 4]
AFTER_STEP = [1] * 12 + [0, 0] + [2] * 4 + [1] * 8
FREED_AT = {0: 0, 3: 1, 7: 2, 11: 3, 15: 4, 17: 5, 21: 6, 23: 7}
CHUNKS = [3, 4, 0, 1, 2]
NEG = -3.0e38
EMPTY = 1.0e6
CONST = dict(ident=128, eps=1, cos=128, sin=128, dmask=1024, qdec=512, kdec=8, causal=128, below=128,
             iota=16, pairid=8, empty=128, limits=3)
OFF, _o = {}, 0
for _k, _v in CONST.items():
    OFF[_k] = _o
    _o += _v
N_CONST = _o
N_FIRST = CONST["ident"] + CONST["eps"]


def build(nc, a, out):
    f32, f32r, bf16 = mybir.dt.float32, mybir.dt.float32r, mybir.dt.bfloat16
    i32, u32 = mybir.dt.int32, mybir.dt.uint32
    ACT, ALU, AX = mybir.ActivationFunctionType, mybir.AluOpType, mybir.AxisListType
    ctx = ExitStack()
    with ctx:
        def sb(name, shape, dt=f32, scope=ctx):
            return scope.enter_context(nc.sbuf_tensor(name, shape, dt))

        x = sb("x", [128, NT, D])
        stage = sb("stage", [128, NS, D])
        w_hi = sb("w_hi", [128, NW, D], f32r)
        w_lo = sb("w_lo", [128, NW, D], f32r)
        with ExitStack() as part:
            hT_hi = sb("hT_hi", [128, KT, SEQ], f32r, scope=part)
            hT_lo = sb("hT_lo", [128, KT, SEQ], f32r, scope=part)
        early = sb("early", [128, NS, D])
        act = sb("act", [128, NT, D])
        gvec = sb("gvec", [128, D])
        con = sb("con", [128, N_CONST])
        g_ret = sb("g_ret", [128, H * 128])
        g_head = sb("g_head", [128, 4, DH])
        r_bias = sb("r_bias", [128, 4 + E_N])
        wr = sb("wr", [128, KT, 20])
        wr_s = sb("wr_s", [128, KT, 40], f32r)
        ss = sb("ss", [128, 16])
        rstd = sb("rstd", [128, 16])
        ssq = sb("ssq", [128, 32 + 16 + 8])
        rstdq = sb("rstdq", [128, 56])
        ssr = sb("ssr", [128, 16])
        rstdr = sb("rstdr", [128, 16])
        mx = sb("mx", [128, 2])
        nmx = sb("nmx", [128, 2, 2])
        rsum = sb("rsum", [128, NT, 8])
        rinv = sb("rinv", [128, NT, 8])
        lg = sb("lg", [128, NT, 20])
        gp = sb("gp", [128, NT, 8])
        ep = sb("ep", [128, NT, 8])
        top = sb("top", [128, NT, 8])
        topi = sb("topi", [128, NT, 8], u32)
        gnum = sb("gnum", [128, NT])
        gexp = sb("gexp", [128, NT, 4])
        gw = sb("gw", [128, NT])
        oneg = sb("oneg", [128, NT, 4])
        prod = sb("prod", [128, NT, 16])
        td = sb("td", [128, NT])
        te = sb("te", [128, NT])
        wtok = sb("wtok", [128, 2, NT])
        enum = sb("enum", [128, 2, NT])
        one_e = sb("one_e", [128, 2, NT, 16])
        sel = sb("sel", [128, NT, 16], bf16)
        ones_b = sb("ones_b", [128, 128], bf16)
        below_b = sb("below_b", [128, 128], bf16)
        pos = sb("pos", [128, 2, NT])
        row_i = sb("row_i", [128, 2, NT], i32)
        tmpr = sb("tmpr", [128, 4])
        rounds_i = sb("rounds_i", [128, 1], i32)
        tab = sb("tab", [64, 128])
        slot_tok = sb("slot_tok", [128, 64], i32)
        slot_pair = sb("slot_pair", [128, 64], i32)
        pair_f = sb("pair_f", [128, 64])
        tok_f = sb("tok_f", [128, 64])
        tok_now = sb("tok_now", [128, 2, 1], i32)
        pair_now = sb("pair_now", [128, 2, 1], i32)

        def const(name, parts=128):
            return con[0:parts, OFF[name]:OFF[name] + CONST[name]]

        ident = const("ident")
        cos_t = const("cos").rearrange("p (t c) -> p t c", t=NT)
        sin_t = const("sin").rearrange("p (t c) -> p t c", t=NT)
        dmask = const("dmask").rearrange("p (h c) -> p h c", h=H)
        qdec = const("qdec").rearrange("p (g c) -> p g c", g=2)
        kdec = const("kdec").rearrange("p (t h) -> p t h", t=2)
        eps = const("eps")

        with ExitStack() as part:
            pq = {c: sb(f"proj{c}", [128, NT, CH], scope=part) for c in (0, 1, 4, 3)}
            pq[2] = pq[3]
            hd = sb("hd", [128, 3, 2, SEQ], scope=part)
            ckT = sb("ckT", [128, 2, MEM], scope=part)
            probs = sb("probs", [128, 2, 512], scope=part)
            probsT = sb("probsT", [128, 2, 512], scope=part)
            cv = sb("cv", [128, 2, H * DH], scope=part)
        with ExitStack() as part:
            sb("mT_below", [128, NT, CH], scope=part)
            mT_hi = sb("mT_hi", [128, KT, MEM], f32r, scope=part)
            mT_lo = sb("mT_lo", [128, KT, MEM], f32r, scope=part)
        with ExitStack() as part:
            xg = sb("xg", [128, 2, D], scope=part)
            xgT_hi = sb("xgT_hi", [128, 2, KT, 128], f32r, scope=part)
            xgT_lo = sb("xgT_lo", [128, 2, KT, 128], f32r, scope=part)
            sil = sb("sil", [128, FF], scope=part)
            hid = sb("hid", [128, FF], scope=part)
            hidT_hi = sb("hidT_hi", [128, FT, 128], f32r, scope=part)
            hidT_lo = sb("hidT_lo", [128, FT, 128], f32r, scope=part)
            ysb = sb("ysb", [128, 2, D], scope=part)
        ck = probsT
        junk = probs[:, 0, :].bitcast(bf16)
        mem_rows = pq[0][:, :, :].rearrange("p (t a) c -> p t (a c)", t=2)
        g_norm1 = hd[:, 0, :, :].rearrange("p g c -> p (g c)")
        y_rows = [act[:, q, :] for q in range(4)] + \
            [pq[3][:, 2 * q:2 * q + 2, :].rearrange("p a c -> p (a c)") for q in range(2)] + \
            [hd[:, q, :, :].rearrange("p g c -> p (g c)") for q in (1, 2)]
        lgT = probsT[0:40, 0, :]
        sq = act[:, 2, 0:512]
        sqr = probsT
        rot_a, rot_b = act[:, 0, 0:512], act[:, 1, 0:512]
        kd = act[:, 3, 0:512].rearrange("p (t c) -> p t c", t=2)
        qdT = hd[:, 2, :, 0:256]
        state = hd[:, 2, :, 256:512]

        bank = [ctx.enter_context(nc.psum_tensor(f"bank{i}", [128, 512], f32)) for i in range(8)]

        h2_d = nc.dram_tensor("h2_scratch", (SEQ, D), f32).ap()
        tab_d = nc.dram_tensor("slot_table", (E_N * SEQ, 1), f32).ap()
        y_d = nc.dram_tensor("pair_rows", (2 * SEQ, D), f32).ap()

        def sem(name):
            return ctx.enter_context(nc.semaphore(name))

        s_const = sem("s_const")
        s_first_c = sem("s_first_c")
        s_pad = sem("s_pad")
        s_begun = sem("s_begun")
        s_xin = [sem(f"s_xin{t}") for t in range(NT)]
        s_stage = [sem(f"s_stage{i}") for i in range(NS)]
        s_early = [sem(f"s_early{i}") for i in range(NS)]
        s_hi = sem("s_hi")
        s_lo = sem("s_lo")
        s_used = sem("s_used")
        s_x = sem("s_x")
        s_rounds = sem("s_rounds")
        s_arrive = sem("s_arrive")
        s_apart = sem("s_apart")
        s_go = sem("s_go")
        s_out = sem("s_out")
        s_memx = sem("s_memx")
        s_gain = [sem(f"s_gain{i}") for i in range(3)]
        s_small = sem("s_small")
        s_wr = sem("s_wr")
        s_tabi = sem("s_tabi")
        s_h2st = sem("s_h2st")
        s_tabw = sem("s_tabw")
        s_tabr = sem("s_tabr")
        s_xg = [sem(f"s_xg{i}") for i in range(2)]
        s_yst = [sem(f"s_yst{i}") for i in range(2)]
        s_yg = [sem(f"s_yg{i}") for i in range(8)]
        s_first = sem("s_first")
        s_cb = sem("s_cb")
        s_known = sem("s_known")
        s_dve = sem("s_dve")
        s_act = sem("s_act")
        s_pool = sem("s_pool")
        s_wrh = sem("s_wrh")
        s_wrl = sem("s_wrl")
        s_std = sem("s_std")
        s_hm = sem("s_hm")
        s_h1 = sem("s_h1")
        s_tr = sem("s_tr")
        s_trh = sem("s_trh")
        s_trl = sem("s_trl")
        s_mkv = sem("s_mkv")
        s_mkve = sem("s_mkve")
        s_proj = sem("s_proj")
        s_pev = sem("s_pev")
        s_ssq = sem("s_ssq")
        s_stdq = sem("s_stdq")
        s_qn = sem("s_qn")
        s_tq = sem("s_tq")
        s_tqe = sem("s_tqe")
        s_rot = sem("s_rot")
        s_kd = sem("s_kd")
        s_s = sem("s_s")
        s_mx = sem("s_mx")
        s_exp = sem("s_exp")
        s_pt = sem("s_pt")
        s_pte = sem("s_pte")
        s_pv = sem("s_pv")
        s_yev = sem("s_yev")
        s_st = sem("s_st")
        s_stm = sem("s_stm")
        s_ro = sem("s_ro")
        s_r = sem("s_r")
        s_re = sem("s_re")
        s_qd = sem("s_qd")
        s_rsq = sem("s_rsq")
        s_ssr = sem("s_ssr")
        s_stdr = sem("s_stdr")
        s_yr = sem("s_yr")
        s_gate = sem("s_gate")
        s_wo = sem("s_wo")
        s_xo = sem("s_xo")
        s_h2 = sem("s_h2")
        s_lgt = sem("s_lgt")
        s_lgc = sem("s_lgc")
        s_lg = sem("s_lg")
        s_ge = sem("s_ge")
        s_gex = sem("s_gex")
        s_td = sem("s_td")
        s_te = sem("s_te")
        s_sel = sem("s_sel")
        s_cnt = sem("s_cnt")
        s_row = sem("s_row")
        s_tabt = sem("s_tabt")
        s_slot = sem("s_slot")
        s_xgt = sem("s_xgt")
        s_xgh = sem("s_xgh")
        s_xgl = sem("s_xgl")
        s_gu = sem("s_gu")
        s_sil = sem("s_sil")
        s_hid = sem("s_hid")
        s_ht = sem("s_ht")
        s_hth = sem("s_hth")
        s_htl = sem("s_htl")
        s_y = sem("s_y")
        s_ye = sem("s_ye")
        s_yfree = sem("s_yfree")
        s_cmb = sem("s_cmb")
        s_pair = sem("s_pair")
        s_last = sem("s_last")

        block = ctx.enter_context(nc.Block())

        class Chain:
            def __init__(self, eng, s):
                self.eng, self.s, self.n = eng, s, 0

            def __call__(self, ins):
                self.n += 1
                ins.then_inc(self.s, 1)
                self.eng.wait_ge(self.s, self.n)

        def bc(ap, shape):
            return ap.to_broadcast(shape)

        def apart(eng):
            eng.sem_inc(s_apart, 1)

        def early_unit(n):
            return early[:, n - EARLY.start, :]

        def turns(eng, body):
            with eng.Fori(0, TURN_E) as pair:
                body(pair, False)
            body(TURN_E, True)
            with eng.Fori(TURN_E + 1, PAIRS) as pair:
                body(pair, False)

        def held(eng, v):
            return v if isinstance(v, int) else eng.snap(v)

        def make_hi(eng, at, n):
            base, loads, aside = at
            if aside and n in EARLY:
                src = early_unit(n)
            else:
                beside = NS if aside and n >= EARLY.stop else 0
                eng.wait_ge(s_stage[n % NS], loads + 16 * ((n - beside) // NS + 1))
                src = stage[:, n % NS, :]
            eng.wait_ge(s_used, base + n + 1)
            eng.activation(w_hi[:, n % NW, :], src, ACT.Copy).then_inc(s_hi, 1)

        def make_lo(eng, base, n, aside=False):
            src = early_unit(n) if aside and n in EARLY else stage[:, n % NS, :]
            eng.wait_ge(s_hi, base + n + 1)
            eng.tensor_tensor(w_lo[:, n % NW, :], src,
                              w_hi[:, n % NW, :].bitcast(f32), ALU.subtract).then_inc(s_lo, 1)

        def rounds_of(eng):
            return eng.value_load(rounds_i[0:1, 0:1], min_val=1, max_val=NT)

        def meet(eng, p):
            eng.sem_inc(s_arrive, 1)
            eng.wait_ge(s_go, p + 1)

        @block.sync
        def _(sp):
            passes = sp.alloc_register("sp_passes")
            sp.reg_mov(passes, 0)

            def load(base, n, src, split=2, aside=False):
                if aside and n in EARLY:
                    return
                former = 2 * NS if aside and EARLY.stop <= n < EARLY.stop + NS else NS
                sp.wait_ge(s_lo, base + (n + 1 + NS - former))
                apart(sp)
                dst = stage[:, n % NS, :].rearrange("p (k c) -> p k c", k=split)
                sp.dma_start(dst, src).then_inc(s_stage[n % NS], 16)

            def tiles(w, row, col):
                return w[row:row + 256, col:col + CH].rearrange("(k p) c -> p k c", p=128)

            def load_pass(base0, first):
                gate, up = (a[k].rearrange("l e d f -> (l e) d f") for k in ("w_exp_gate", "w_exp_up"))
                down = a["w_exp_down"].rearrange("l e f d -> (l e) f d")

                def gate_up_unit(e, k):
                    src = (gate, up)[k % 2][bass.ds(e, 1), (k // 2) * 256:(k // 2 + 1) * 256, :]
                    return src.rearrange("o (k p) c -> p (o k) c", p=128)

                def down_unit(e, k):
                    return down[bass.ds(e, 1), k * 128:(k + 1) * 128, :].rearrange("o p c -> p o c")

                def gate_up(base, e, n, first, aside=False):
                    for k in range(first, first + 4):
                        load(base, n + k - first, gate_up_unit(e, k), aside=aside)

                def downs(base, e, n, aside=False):
                    for k in range(FT):
                        load(base, n + k, down_unit(e, k), split=1, aside=aside)

                def step(base, e, n, aside=False):
                    gate_up(base, e, n, 0, aside)
                    downs(base, e - 1, n + 4, aside)
                    gate_up(base, e, n + 8, 4, aside)

                gate_up(base0, flat[0], 0, 0)
                gate_up(base0, flat[0], 4, 4)
                if first:
                    sp.wait_ge(s_lg, 1)
                e = sp.snap(flat[0] + (2 * TURN_E + 1))
                units = [(gate_up_unit(e, 3), 2)] + [(down_unit(e - 1, k), 1) for k in range(FT)] + \
                    [(gate_up_unit(e, k), 2) for k in (4, 5, 6)]
                for k, (src, split) in enumerate(units):
                    sp.dma_start(early[:, k, :].rearrange("p (k c) -> p k c", k=split), src)\
                        .then_inc(s_early[k], 16)

                def turn(pair, aside):
                    base = sp.snap(base0 + pair * (2 * U_E))
                    for i in range(2):
                        step(base, sp.snap(flat[0] + pair * 2 + (i + 1)), U_FIRST + U_E * i, aside)

                turns(sp, turn)
                end = sp.snap(base0 + PAIRS * 2 * U_E)
                step(end, sp.snap(flat[0] + (E_N - 1)), U_FIRST)
                downs(end, sp.snap(flat[0] + (E_N - 1)), U_FIRST + U_E)

            flat = [None]
            sp.dma_start(con[:, 0:N_FIRST], a["const_pack"][:, 0:N_FIRST]).then_inc(s_first_c, 16)
            sp.wait_ge(s_begun, 1)
            with sp.Fori(0, DEPTH) as layer:
                p = sp.snap(passes, min_val=0, max_val=NT * DEPTH)
                base = sp.snap(layer * U_ATT + p * U_PASS)

                def of(w, r, c):
                    return w[bass.ds(layer, 1), r:r + 256, c:c + CH].rearrange("o (k p) c -> p (o k) c", p=128)

                for n in range(U_MEM):
                    load(base, n, of(a["w_mem_kv"], 256 * n, 0))
                with sp.If(layer < 1):
                    for t in range(NT):
                        sp.dma_start(x[:, t, :], a["x"][0, t * 128:(t + 1) * 128, :]).then_inc(s_xin[t], 16)
                    sp.dma_start(con[:, N_FIRST:], a["const_pack"][:, N_FIRST:]).then_inc(s_const, 16)
                with sp.Else():
                    sp.nop()
                for q, c in enumerate(CHUNKS):
                    for n in range(4):
                        load(base, U_MEM + 4 * q + n, of(a["w_in"], 256 * n, CH * c))
                for q in range(2):
                    for n in range(4):
                        load(base, U_MEM + U_PROJ + 4 * q + n, of(a["w_out"], 256 * n, CH * q))
                flat[0] = sp.snap(layer * E_N)
                load_pass(sp.snap(layer * U_ATT + U_ATT + p * U_PASS), True)
                sp.reg_add(passes, passes, 1)
                sp.wait_ge(s_rounds, layer + 1)
                apart(sp)
                rounds = rounds_of(sp)
                with sp.If(rounds > 1):
                    with sp.Fori(1, rounds) as r:
                        p2 = sp.snap(passes, min_val=1, max_val=NT * DEPTH)
                        load_pass(sp.snap(layer * U_ATT + U_ATT + p2 * U_PASS), False)
                        sp.reg_add(passes, passes, 1)
                with sp.Else():
                    sp.nop()
            for t in range(NT):
                sp.wait_ge(s_x, 16 * DEPTH + 4 * (t + 1))
                sp.dma_start(out[0, t * 128:(t + 1) * 128, :], x[:, t, :]).then_inc(s_out, 16)
            sp.wait_ge(s_out, 16 * NT)

        @block.gpsimd
        def _(pool):
            def load_memory():
                pool.dma_start(mem_rows, a["mem"][0].rearrange("(t p) d -> p t d", p=128)).then_inc(s_memx, 16)

            load_memory()
            pool.sem_inc(s_begun, 1)
            pool.memset(gp[:, :, :], NEG).then_inc(s_pad, 1)
            pool.memset(ep[:, :, :], NEG).then_inc(s_pad, 1)
            passes = pool.alloc_register("pool_passes")
            pool.reg_mov(passes, 0)

            def load_results():
                for q in range(2 * NT):
                    r0 = SEQ * (q % 2) + 128 * (q // 2)
                    pool.dma_start(y_rows[q], y_d[r0:r0 + 128, :]).then_inc(s_yg[q], 16)

            with pool.Fori(0, DEPTH) as layer:
                chain = Chain(pool, s_pool)

                def row(w):
                    return w[bass.ds(layer, 1), :].rearrange("o n -> (o n)").partition_broadcast(128)

                pool.dma_start(gvec[:, :], row(a["mem_norm_g"])).then_inc(s_gain[0], 16)
                pool.dma_start(g_norm1, row(a["norm1_g"])).then_inc(s_gain[1], 16)
                with pool.If(layer > 0):
                    load_results()
                with pool.Else():
                    pool.nop()
                pool.wait_ge(s_const, 16)
                pool.dma_start(g_ret[:, :], row(a["ret_norm_g"].rearrange("l h v -> l (h v)"))).then_inc(s_small, 16)
                for i, name in enumerate(("moba_qn_g", "moba_kn_g", "mem_qn_g", "mem_kn_g")):
                    pool.dma_start(g_head[:, i, :], row(a[name])).then_inc(s_small, 16)
                pool.dma_start(r_bias[:, 0:4], row(a["b_router_grp"])).then_inc(s_small, 16)
                pool.dma_start(r_bias[:, 4:20], row(a["b_router_exp"])).then_inc(s_small, 16)
                for lo_c, hi_c, name in ((0, 4, "w_router_grp"), (4, 20, "w_router_exp")):
                    pool.dma_start(wr[:, :, lo_c:hi_c], a[name][bass.ds(layer, 1), :, :]
                                   .rearrange("o (k p) e -> p (o k) e", p=128)).then_inc(s_wr, 16)
                pool.dma_start(tab_d.rearrange("(n q) o -> n (q o)", q=128), const("empty", 64)).then_inc(s_tabi, 16)
                pool.wait_ge(s_hm, 2)
                pool.dma_start(gvec[:, :], row(a["norm2_g"])).then_inc(s_gain[2], 16)

                pool.wait_ge(s_pev, 12)
                pool.wait_ge(s_tr, 12)
                for t in range(NT):
                    v = pq[0][:, t, :].rearrange("p (h s c) -> p h s c", h=8, s=2)
                    va = rot_a.rearrange("p (h s c) -> p h s c", h=8, s=2)
                    vb = rot_b.rearrange("p (h s c) -> p h s c", h=8, s=2)
                    v16 = pq[0][:, t, :].rearrange("p (g c) -> p g c", g=16)
                    a16 = rot_a.rearrange("p (g c) -> p g c", g=16)
                    b16 = rot_b.rearrange("p (g c) -> p g c", g=16)
                    chain(pool.tensor_tensor(a16, v16, bc(cos_t[:, t, :].unsqueeze(1), [128, 16, 32]), ALU.mult))
                    chain(pool.tensor_tensor(b16, v16, bc(sin_t[:, t, :].unsqueeze(1), [128, 16, 32]), ALU.mult))
                    chain(pool.tensor_tensor(v[:, :, 0, :], va[:, :, 0, :], vb[:, :, 1, :], ALU.subtract))
                    chain(pool.tensor_tensor(v[:, :, 1, :], vb[:, :, 0, :], va[:, :, 1, :], ALU.add))
                pool.sem_inc(s_rot, 1)
                for t in range(2):
                    pool.tensor_tensor(kd[:, t, :].rearrange("p (h c) -> p h c", h=H),
                                       pq[0][:, t, 256:512].rearrange("p (h c) -> p h c", h=H),
                                       bc(kdec[:, t, :].unsqueeze(2), [128, H, DH]), ALU.mult).then_inc(s_kd, 1)

                for t in range(NT):
                    pool.wait_ge(s_pev, 17 + t)
                    pool.tensor_tensor(pq[2][:, t, :], pq[2][:, t, :], g_ret[:, :], ALU.mult).then_inc(s_gate, 1)

                for t in range(NT):
                    pool.wait_ge(s_h2, t + 1)
                    pool.dma_start(h2_d[t * 128:(t + 1) * 128, :], act[:, t, :]).then_inc(s_h2st, 16)
                pool.wait_ge(s_tabi, layer * 16 + 16)
                apart(pool)
                for q in range(2):
                    pool.wait_ge(s_row, q + 1)
                    for t in range(NT):
                        pool.indirect_dma_start(
                            out=tab_d, out_offset=bass.IndirectOffsetOnAxis(ap=row_i[:, q, t:t + 1], axis=0),
                            in_=const("pairid")[:, NT * q + t:NT * q + t + 1], in_offset=None).then_inc(s_tabw, 16)
                pool.wait_ge(s_tabw, layer * 128 + 128)
                apart(pool)
                pool.dma_start(tab[:, :], tab_d.rearrange("(n q) o -> n (q o)", q=128)).then_inc(s_tabr, 16)
                pool.wait_ge(s_h2st, layer * 64 + 64)
                apart(pool)
                pool.wait_ge(s_slot, 1)
                pool.wait_ge(s_known, 1)
                rounds = rounds_of(pool)
                with pool.Fori(0, rounds) as r:
                    p = pool.snap(passes, min_val=0, max_val=NT * DEPTH)

                    def gather(i, col):
                        pool.tensor_copy(tok_now[:, i, :], slot_tok[:, bass.ds(col, 1)]).then_inc(s_last, 1)

                    def gather_dma(i):
                        pool.indirect_dma_start(
                            out=xg[:, i, :], out_offset=None, in_=h2_d,
                            in_offset=bass.IndirectOffsetOnAxis(ap=tok_now[:, i, :], axis=0),
                            bounds_check=SEQ - 1, oob_is_err=False).then_inc(s_xg[i], 16)

                    def scatter(i, e2, pair16, col):
                        pool.wait_ge(s_ye, e2 + (i + 2))
                        pool.tensor_copy(pair_now[:, i, :], slot_pair[:, bass.ds(col, 1)]).then_inc(s_pair, 1)
                        pool.wait_ge(s_pair, e2 + (i + 1))
                        apart(pool)
                        pool.indirect_dma_start(
                            out=y_d, out_offset=bass.IndirectOffsetOnAxis(ap=pair_now[:, i, :], axis=0),
                            in_=ysb[:, i, :], in_offset=None,
                            bounds_check=2 * SEQ - 1, oob_is_err=False).then_inc(s_yst[i], 16)
                        pool.wait_ge(s_yst[i], pair16 + 16)
                        pool.sem_inc(s_yfree, 1)

                    pool.sem_inc(s_yfree, 2)
                    pool.wait_ge(s_memx, p * 16 + 16)
                    for i in range(2):
                        gather(i, r + 4 * i)
                        pool.wait_ge(s_last, i + 1)
                        gather_dma(i)
                    with pool.Fori(0, E_N // 2 - 1) as pair:
                        e2 = pool.snap(pair * 2)
                        for i in range(2):
                            pool.wait_ge(s_xgt, e2 + (i + 1))
                            gather(i, pair * 8 + r + (8 + 4 * i))
                            pool.wait_ge(s_last, e2 + (i + 3))
                            apart(pool)
                            gather_dma(i)
                            scatter(i, e2, p * 128 + pair * 16, pair * 8 + r + 4 * i)
                    scatter(0, E_N - 2, p * 128 + (8 * E_N - 16), r + 4 * (E_N - 2))
                    pool.wait_ge(s_xgt, E_N)
                    load_memory()
                    scatter(1, E_N - 2, p * 128 + (8 * E_N - 16), r + 4 * (E_N - 1))
                    pool.wait_ge(s_arrive, p * 3 + 3)
                    apart(pool)
                    pool.sem_clear(range(s_first.num, s_last.num + 1))
                    pool.sem_inc(s_go, 1)
                    pool.reg_add(passes, passes, 1)
            load_results()

        @block.scalar
        def _(sc):
            sc.wait_ge(s_first_c, 16)
            passes = sc.alloc_register("act_passes")
            sc.reg_mov(passes, 0)

            loaded = sc.alloc_register("act_loaded")
            sc.reg_mov(loaded, 0)
            per_unit = 16 // NS

            def ring():
                return sc.snap(loaded, min_val=0, max_val=per_unit * DEPTH * (U_ATT + NT * U_PASS))

            with sc.Fori(0, DEPTH) as layer:
                p = sc.snap(passes, min_val=0, max_val=NT * DEPTH)
                base = sc.snap(layer * U_ATT + p * U_PASS), ring(), False
                chain = Chain(sc, s_act)

                def squares(src, col):
                    chain(sc.activation(junk, src, ACT.Square, accum_out=ss[:, col:col + 1]))

                def root(dst, src, n, s):
                    sc.activation(dst, src, ACT.Sqrt, bias=eps, scale=1.0 / n).then_inc(s, 1)

                def bank_hi(j, b, dst):
                    sc.wait_ge(s_tr, j + 1)
                    sc.activation(dst, bank[b][:, :].rearrange("p (k c) -> p k c", k=4), ACT.Copy).then_inc(s_trh, 1)

                sc.wait_ge(s_memx, p * 16 + 16)
                for t in range(2):
                    squares(mem_rows[:, t, :], t)
                root(rstd[:, 0:2], ss[:, 0:2], D, s_std)
                for n in range(2):
                    make_hi(sc, base, n)
                for j in range(4):
                    bank_hi(j, j, mT_hi[:, 4 * (j % 2):4 * (j % 2) + 4, 128 * (j // 2):128 * (j // 2) + 128])
                for n in range(2, 4):
                    make_hi(sc, base, n)
                for t in range(NT):
                    sc.wait_ge(s_x, layer * 16 + 4 * (t + 1))
                    squares(x[:, t, :], 2 + t)
                    root(rstd[:, 2 + t:3 + t], ss[:, 2 + t:3 + t], D, s_std)
                for k in range(4):
                    make_hi(sc, base, 4 + k)
                    for j in (2 * k, 2 * k + 1):
                        bank_hi(4 + j, (6, 7, 0, 1, 2, 3, 6, 7)[j],
                                hT_hi[:, 4 * (j % 2):4 * (j % 2) + 4, 128 * k:128 * k + 128])
                for t in range(2):
                    sc.wait_ge(s_mkv, 1)
                    sc.activation(ck[:, t, 0:256], bank[4 + t][:, 0:256], ACT.Copy)
                    sc.activation(cv[:, t, :], bank[4 + t][:, 256:512], ACT.Copy).then_inc(s_mkve, 1)
                sc.wait_ge(s_wr, layer * 32 + 32)
                sc.activation(wr_s[:, :, 0:20], wr[:, :, :], ACT.Copy).then_inc(s_wrh, 1)

                def evacuate(n):
                    for t in range(NT):
                        sc.wait_ge(s_proj, 4 * n + t + 1)
                        sc.activation(pq[CHUNKS[n]][:, t, :], bank[CHUNK_BANK[n] + t][:, :],
                                      ACT.Silu if CHUNKS[n] == 2 else ACT.Copy).then_inc(s_pev, 1)

                for n in range(3):
                    for k in range(4):
                        make_hi(sc, base, 8 + 4 * n + k)
                    if n:
                        sc.wait_ge(s_ssq, n)
                        part_ = slice(0, 32) if n == 1 else slice(32, 56)
                        root(rstdq[:, part_], ssq[:, part_], DH, s_stdq)
                    evacuate(n)
                for j in range(24):
                    t, q = j // 6, j % 6
                    sc.wait_ge(s_mx, j + 1)
                    if j >= 2:
                        sc.wait_ge(s_pt, j - 1)
                    if q < 2:
                        for g in range(2):
                            ins = sc.activation(probs[:, j % 2, 256 * g:256 * g + 256],
                                                bank[j % 2][:, 256 * g:256 * g + 256], ACT.Exp,
                                                bias=nmx[:, j % 2, g:g + 1], scale=DH ** -0.5,
                                                accum_out=rsum[:, t, 4 + q + 2 * g:5 + q + 2 * g])
                    else:
                        w = 128 * (t + 1)
                        ins = sc.activation(probs[:, j % 2, 0:w], bank[j % 2][:, 0:w], ACT.Exp,
                                            bias=nmx[:, j % 2, 0:1], scale=DH ** -0.5,
                                            accum_out=rsum[:, t, q - 2:q - 1])
                    ins.then_inc(s_exp, 1)
                    if j in FREED_AT:
                        make_hi(sc, base, 20 + FREED_AT[j])
                    if j == 11:
                        evacuate(3)
                evacuate(4)
                for t in range(NT):
                    sc.wait_ge(s_ro, H * (t // 2 + 1))
                    if t >= 2:
                        sc.wait_ge(s_ssr, t - 1)
                    sc.activation(sqr[:, t % 2, :], bank[(2, 3, 6, 7)[t]][:, :], ACT.Square).then_inc(s_rsq, 1)
                    if t % 2:
                        sc.wait_ge(s_ssr, t + 1)
                        root(rstdr[:, 4 * t - 4:4 * t + 4], ssr[:, 4 * t - 4:4 * t + 4], 128, s_stdr)
                for j in range(8):
                    bank_hi(12 + j, (0, 1, 4, 5)[j % 4],
                            hT_hi[:, 4 * (j % 2):4 * (j % 2) + 4, 128 * (j // 2):128 * (j // 2) + 128])
                for k in range(4):
                    make_hi(sc, base, 28 + k)
                for t in range(NT):
                    sc.wait_ge(s_xo, 5 + t)
                    squares(x[:, t, :], 6 + t)
                    root(rstd[:, 6 + t:7 + t], ss[:, 6 + t:7 + t], D, s_std)
                for j in range(8):
                    bank_hi(20 + j, (2, 3, 6, 7, 0, 1, 4, 5)[j],
                            hT_hi[:, 4 * (j % 2):4 * (j % 2) + 4, 128 * (j // 2):128 * (j // 2) + 128])
                sc.wait_ge(s_ge, 1)
                sc.activation(gexp[:, :, :], gexp[:, :, :], ACT.Exp).then_inc(s_gex, 1)
                sc.wait_ge(s_td, 1)
                sc.activation(te[:, :], td[:, :], ACT.Exp).then_inc(s_te, 1)

                sc.reg_add(loaded, loaded, U_ATT * per_unit)
                sc.wait_ge(s_known, 1)
                rounds = rounds_of(sc)
                with sc.Fori(0, rounds) as r:
                    p2 = sc.snap(passes, min_val=0, max_val=NT * DEPTH)
                    base_p = sc.snap(layer * U_ATT + U_ATT + p2 * U_PASS), ring(), False
                    sc.sem_inc(s_ye, 1)
                    for n in range(3):
                        make_hi(sc, base_p, n)

                    def rows_hi(i, count):
                        sc.wait_ge(s_xgt, count)
                        for q in range(2):
                            ins = sc.activation(xgT_hi[:, i, 4 * q:4 * q + 4, :],
                                                bank[4 + q][:, :].rearrange("p (k c) -> p k c", k=4), ACT.Copy)
                        ins.then_inc(s_xgh, 1)

                    def hidden_hi(m):
                        sc.wait_ge(s_ht, m)
                        sc.activation(hidT_hi[:, :, :], bank[4][:, :].rearrange("p (k c) -> p k c", k=4),
                                      ACT.Copy).then_inc(s_hth, 1)

                    def silu(m, i):
                        sc.wait_ge(s_gu, m)
                        sc.activation(sil[:, :], bank[(0, 6)[1 - i]][:, :], ACT.Silu).then_inc(s_sil, 1)

                    def results(m, i):
                        sc.wait_ge(s_y, m)
                        sc.wait_ge(s_yfree, m)
                        for q in range(2):
                            ins = sc.activation(ysb[:, 1 - i, 512 * q:512 * q + 512], bank[2 + q][:, :], ACT.Copy)
                        ins.then_inc(s_ye, 1)

                    def step(m, i, base_e, n0, last=False):
                        silu(m, i)
                        make_hi(sc, base_e, n0 + 3)
                        hidden_hi(m)
                        for n in range(4, 11):
                            make_hi(sc, base_e, n0 + n)
                        results(m, i)
                        make_hi(sc, base_e, n0 + 11)
                        if not last:
                            rows_hi(1 - i, m + 2)
                        for n in range(3):
                            make_hi(sc, base_e, n0 + U_E + n)

                    rows_hi(0, 1)
                    for n in range(3, U_FIRST):
                        make_hi(sc, base_p, n)
                    rows_hi(1, 2)
                    for n in range(3):
                        make_hi(sc, base_p, U_FIRST + n)

                    passed = [0]

                    def turn(pair, aside):
                        base_e = sc.snap(base_p[0] + pair * (2 * U_E)), \
                            sc.snap(base_p[1] + (pair * (2 * U_E * per_unit) - passed[0])), aside
                        if aside:
                            for k in range(NS):
                                sc.wait_ge(s_early[k], p2 * 16 + 16)
                            passed[0] = 16
                        for k in range(2):
                            step(held(sc, pair * 2 + (k + 1)), (k + 1) % 2, base_e, U_FIRST + U_E * k)

                    turns(sc, turn)
                    end = sc.snap(base_p[0] + PAIRS * 2 * U_E), \
                        sc.snap(base_p[1] + (PAIRS * 2 * U_E * per_unit - passed[0])), False
                    step(E_N - 1, 1, end, U_FIRST, last=True)
                    silu(E_N, 0)
                    make_hi(sc, end, U_FIRST + U_E + 3)
                    hidden_hi(E_N)
                    results(E_N, 0)
                    sc.wait_ge(s_ye, E_N + 1)
                    meet(sc, p2)
                    sc.reg_add(loaded, loaded, (U_PASS - NS) * per_unit)
                    sc.reg_add(passes, passes, 1)

        @block.vector
        def _(dv):
            dv.sem_inc(s_lo, NS)
            dv.wait_ge(s_pad, 2)
            passes = dv.alloc_register("dve_passes")
            dv.reg_mov(passes, 0)

            def combine(loaded, t):
                for q in (2 * t, 2 * t + 1):
                    dv.wait_ge(s_yg[q], loaded)
                    dv.scalar_tensor_tensor(out=x[:, t, :], in0=y_rows[q], scalar=wtok[:, q % 2, t:t + 1],
                                            in1=x[:, t, :], op0=ALU.mult, op1=ALU.add).then_inc(s_cmb, 1)
                    dv.wait_ge(s_cmb, q + 1)
                    if q % 2:
                        dv.sem_inc(s_x, 4)

            with dv.Fori(0, DEPTH) as layer:
                p = dv.snap(passes, min_val=0, max_val=NT * DEPTH)
                base = dv.snap(layer * U_ATT + p * U_PASS)
                chain = Chain(dv, s_dve)
                iota = const("iota")

                def bank_lo(j, b, dst, hi):
                    dv.wait_ge(s_trh, j + 1)
                    dv.tensor_tensor(dst, bank[b][:, :].rearrange("p (k c) -> p k c", k=4), hi.bitcast(f32),
                                     ALU.subtract).then_inc(s_trl, 1)

                def hT_part(h, j):
                    return h[:, 4 * (j % 2):4 * (j % 2) + 4, 128 * (j // 2):128 * (j // 2) + 128]

                def norm(dst, src, col, s, gain):
                    dv.scalar_tensor_tensor(out=dst, in0=src, scalar=rstd[:, col:col + 1], in1=gain,
                                            op0=ALU.mult, op1=ALU.mult).then_inc(s, 1)

                dv.wait_ge(s_std, 1)
                chain(dv.reciprocal(rstd[:, 0:2], rstd[:, 0:2]))
                dv.wait_ge(s_gain[0], layer * 16 + 16)
                for t in range(2):
                    norm(mem_rows[:, t, :], mem_rows[:, t, :], t, s_hm, gvec[:, :])
                for n in range(2):
                    make_lo(dv, base, n)
                for j in range(4):
                    bank_lo(j, j, hT_part(mT_lo, j), hT_part(mT_hi, j))
                for n in range(2, 4):
                    make_lo(dv, base, n)
                dv.wait_ge(s_gain[1], layer * 16 + 16)
                apart(dv)

                def norm_x(t):
                    dv.wait_ge(s_std, 2 + t)
                    chain(dv.reciprocal(rstd[:, 2 + t:3 + t], rstd[:, 2 + t:3 + t]))
                    norm(act[:, t, :], x[:, t, :], 2 + t, s_h1, g_norm1)

                steps = chain.n
                with dv.If(layer > 0):
                    before = dv.snap(layer * 16, min_val=16, max_val=16 * DEPTH)
                    for t in range(NT):
                        combine(before, t)
                        if t:
                            norm_x(t - 1)
                with dv.Else():
                    chain.n = steps
                    for t in range(NT):
                        dv.wait_ge(s_xin[t], 16)
                        dv.sem_inc(s_x, 4)
                        if t:
                            norm_x(t - 1)
                norm_x(NT - 1)
                for k in range(4):
                    make_lo(dv, base, 4 + k)
                    for j in (2 * k, 2 * k + 1):
                        bank_lo(4 + j, (6, 7, 0, 1, 2, 3, 6, 7)[j], hT_part(hT_lo, j), hT_part(hT_hi, j))
                dv.wait_ge(s_wrh, 1)
                dv.tensor_tensor(wr_s[:, :, 20:40], wr[:, :, :], wr_s[:, :, 0:20].bitcast(f32), ALU.subtract)\
                    .then_inc(s_wrl, 1)

                def head_squares(src, heads, dst):
                    v = sq[:, 0:heads * DH]
                    chain(dv.tensor_tensor(v, src, src, ALU.mult))
                    chain(dv.tensor_reduce(dst, v.rearrange("p (h c) -> p h c", h=heads), axis=AX.X, op=ALU.add))

                def head_norm(v, heads, col, gains):
                    v3 = v.rearrange("p (h c) -> p h c", h=heads)
                    chain(dv.tensor_tensor(v3, v3, bc(rstdq[:, col:col + heads].unsqueeze(2), [128, heads, DH]),
                                           ALU.mult))
                    n = heads // len(gains)
                    for q, g in enumerate(gains):
                        part_ = v3[:, q * n:(q + 1) * n, :]
                        chain(dv.tensor_tensor(part_, part_, bc(g_head[:, g, :].unsqueeze(1), [128, n, DH]), ALU.mult))

                def heads_out(j, b, dst):
                    dv.wait_ge(s_tq, j + 1)
                    dv.tensor_copy(dst, bank[b][:, :]).then_inc(s_tqe, 1)

                dv.wait_ge(s_small, layer * 112 + 112)
                dv.wait_ge(s_const, 16)
                dv.tensor_copy(below_b[:, :], const("below")).then_inc(s_cb, 1)
                dv.memset(ones_b[:, :], 1.0).then_inc(s_cb, 1)
                for n in range(3):
                    for k in range(4):
                        make_lo(dv, base, 8 + 4 * n + k)
                    if n == 0:
                        for t in range(NT):
                            dv.wait_ge(s_pev, t + 1)
                            head_squares(pq[3][:, t, :], 8, ssq[:, 8 * t:8 * t + 8])
                        dv.sem_inc(s_ssq, 1)
                    if n == 1:
                        dv.wait_ge(s_mkve, 2)
                        for t in range(2):
                            head_squares(ck[:, t, 0:256], 4, ssq[:, 48 + 4 * t:52 + 4 * t])
                        for t in range(NT):
                            dv.wait_ge(s_pev, 4 + t + 1)
                            head_squares(pq[4][:, t, 256:512], 4, ssq[:, 32 + 4 * t:36 + 4 * t])
                        dv.sem_inc(s_ssq, 1)
                        dv.wait_ge(s_stdq, 1)
                        chain(dv.reciprocal(rstdq[:, 0:32], rstdq[:, 0:32]))
                        for t in range(NT):
                            head_norm(pq[3][:, t, :], 8, 8 * t, (0, 1))
                    if n == 2:
                        dv.wait_ge(s_stdq, 2)
                        chain(dv.reciprocal(rstdq[:, 32:56], rstdq[:, 32:56]))
                        for t in range(2):
                            head_norm(ck[:, t, 0:256], 4, 48 + 4 * t, (3,))
                        for t in range(NT):
                            head_norm(pq[4][:, t, 256:512], 4, 32 + 4 * t, (2,))
                        dv.sem_inc(s_qn, 1)
                heads_out(0, 0, ckT[:, :, :].rearrange("p g c -> p (g c)"))
                for j in range(1, 7):
                    heads_out(j, j % 4, hd[:, (j - 1) // 2, (j - 1) % 2, :])

                def probs_out(j):
                    dv.wait_ge(s_pt, j + 1)
                    if j >= 2:
                        dv.wait_ge(s_pv, j - 1)
                    w = 512 if j % 6 < 2 else 128 * (j // 6 + 1)
                    dv.tensor_copy(probsT[:, j % 2, 0:w], bank[2][:, 0:w]).then_inc(s_pte, 1)

                def tile_out(t):
                    dv.wait_ge(s_pv, 6 * t + 6)
                    chain(dv.reciprocal(rinv[:, t, :], rsum[:, t, :]))
                    dv.tensor_tensor(act[:, t, 512:1024].rearrange("p (h c) -> p h c", h=8),
                                     bank[3][:, :].rearrange("p (h c) -> p h c", h=8),
                                     bc(rinv[:, t, :].unsqueeze(2), [128, 8, DH]), ALU.mult).then_inc(s_yev, 1)

                for j in range(24):
                    t, q = j // 6, j % 6
                    dv.wait_ge(s_s, j + 1)
                    if j >= 2:
                        dv.wait_ge(s_exp, j - 1)
                    if q < 2:
                        chain(dv.tensor_reduce(mx[:, 0:2], bank[j % 2][:, :].rearrange("p (g c) -> p g c", g=2),
                                               axis=AX.X, op=ALU.max))
                        dv.tensor_scalar(nmx[:, j % 2, :], mx[:, 0:2], -DH ** -0.5, None, ALU.mult).then_inc(s_mx, 1)
                    else:
                        own = bank[j % 2][:, 128 * t:128 * t + 128]
                        chain(dv.tensor_tensor(own, own, const("causal"), ALU.add))
                        chain(dv.tensor_reduce(mx[:, 0:1], bank[j % 2][:, 0:128 * (t + 1)], axis=AX.X, op=ALU.max))
                        dv.tensor_scalar(nmx[:, j % 2, 0:1], mx[:, 0:1], -DH ** -0.5, None, ALU.mult)\
                            .then_inc(s_mx, 1)
                    dv.wait_ge(s_mx, j + 1)
                    if j >= 1:
                        probs_out(j - 1)
                    if j >= 7 and j % 6 == 1:
                        tile_out(j // 6 - 1)
                    if j - 1 in FREED_AT:
                        make_lo(dv, base, 20 + FREED_AT[j - 1])
                probs_out(23)
                make_lo(dv, base, 20 + FREED_AT[23])
                tile_out(3)

                for j in range(4):
                    heads_out(7 + j, j, hd[:, j // 2, j % 2, :])
                dv.wait_ge(s_tqe, 11)
                chain(dv.memset(state, 0.0))
                dv.tensor_tensor(qdT, hd[:, 0, :, 256:512], qdec, ALU.mult).then_inc(s_qd, 1)
                for r in range(8):
                    h = r % 4
                    dv.wait_ge(s_st, r + 1)
                    if r >= 2:
                        dv.wait_ge(s_ro, r - 1)
                    dv.tensor_tensor(probs[:, r % 2, 0:256], bank[r % 2][:, 0:256], dmask[:, h, :], ALU.mult)
                    dv.tensor_tensor(probs[:, r % 2, 256:384], bank[r % 2][:, 256:384], dmask[:, h, 0:128],
                                     ALU.mult).then_inc(s_stm, 1)
                    if r == 2:
                        dv.wait_ge(s_r, 1)
                        for g in range(2):
                            half = slice(64 * g, 64 * g + 64)
                            ins = dv.tensor_copy(state[half, :, 128 * g:128 * g + 128],
                                                 bank[4][half, 0:256].rearrange("p (g c) -> p g c", g=2))
                        ins.then_inc(s_re, 1)
                dv.wait_ge(s_rot, 1)
                dv.wait_ge(s_gate, NT)
                for c in range(2):
                    for t in (2 * c, 2 * c + 1):
                        dv.wait_ge(s_rsq, t + 1)
                        dv.tensor_reduce(ssr[:, 4 * t:4 * t + 4], sqr[:, t % 2, :].rearrange("p (h c) -> p h c", h=H),
                                         axis=AX.X, op=ALU.add).then_inc(s_ssr, 1)
                    dv.wait_ge(s_stdr, c + 1)
                    part_ = rstdr[:, 8 * c:8 * c + 8]
                    chain(dv.reciprocal(part_, part_))
                    for t in (2 * c, 2 * c + 1):
                        for h in range(H):
                            col = slice(128 * h, 128 * h + 128)
                            ins = dv.scalar_tensor_tensor(
                                out=act[:, t, col], in0=bank[(2, 3, 6, 7)[t]][:, col],
                                scalar=rstdr[:, 4 * t + h:4 * t + h + 1], in1=pq[2][:, t, col],
                                op0=ALU.mult, op1=ALU.mult)
                        ins.then_inc(s_yr, 1)
                for j in range(8):
                    bank_lo(12 + j, (0, 1, 4, 5)[j % 4], hT_part(hT_lo, j), hT_part(hT_hi, j))
                for k in range(4):
                    make_lo(dv, base, 28 + k)
                def residual(n, t):
                    dv.wait_ge(s_wo, 4 * n + t + 1)
                    v = x[:, t, 512 * n:512 * n + 512]
                    dv.tensor_tensor(v, bank[((2, 3, 6, 7), (0, 1, 4, 5))[n][t]][:, :], v, ALU.add)\
                        .then_inc(s_xo, 1)

                def norm2(t):
                    dv.wait_ge(s_std, 6 + t)
                    chain(dv.reciprocal(rstd[:, 6 + t:7 + t], rstd[:, 6 + t:7 + t]))
                    norm(act[:, t, :], x[:, t, :], 6 + t, s_h2, gvec[:, :])

                for t in range(NT):
                    residual(0, t)
                dv.wait_ge(s_gain[2], layer * 16 + 16)
                dv.wait_ge(s_tr, 20)
                for t in range(NT):
                    residual(1, t)
                    if t:
                        norm2(t - 1)
                norm2(NT - 1)
                for j in range(8):
                    bank_lo(20 + j, (2, 3, 6, 7, 0, 1, 4, 5)[j], hT_part(hT_lo, j), hT_part(hT_hi, j))
                for half in range(2):
                    c = slice(256 * half, 256 * half + 256)
                    dv.wait_ge(s_lgt, half + 1)
                    dv.tensor_copy(lgT[:, c], bank[2 + half][0:40, c]).then_inc(s_lgc, 1)
                dv.wait_ge(s_lg, 1)
                logits = bank[6][:, 0:160].rearrange("p (t c) -> p t c", t=NT)
                chain(dv.tensor_copy(lg[:, :, :], logits[:, :, 20:40]))
                chain(dv.tensor_tensor(lg[:, :, :], logits[:, :, 0:20], lg[:, :, :], ALU.add))
                chain(dv.tensor_tensor(lg[:, :, :], lg[:, :, :], bc(r_bias[:, :].unsqueeze(1), [128, NT, 20]),
                                       ALU.add))
                chain(dv.tensor_copy(gp[:, :, 0:4], lg[:, :, 0:4]))
                for t in range(NT):
                    ins = dv.max(top[:, t, :], gp[:, t, :])
                chain(ins)
                for t in range(NT):
                    ins = dv.max_index(topi[:, t, :], top[:, t, :], gp[:, t, :])
                dv.tensor_tensor(gexp[:, :, :], gp[:, :, 0:4], bc(top[:, :, 0:1], [128, NT, 4]), ALU.subtract)\
                    .then_inc(s_ge, 1)
                dv.wait_ge(s_ge, 1)
                chain(dv.tensor_copy(gnum[:, :], topi[:, :, 0]))
                chain(dv.tensor_tensor(oneg[:, :, :], bc(iota[:, 0:4].unsqueeze(1), [128, NT, 4]),
                                       bc(gnum[:, :].unsqueeze(2), [128, NT, 4]), ALU.is_equal))
                p4 = prod[:, :, :].rearrange("p t (g j) -> p t g j", g=4)
                chain(dv.tensor_tensor(p4, lg[:, :, 4:20].rearrange("p t (g j) -> p t g j", g=4),
                                       bc(oneg[:, :, :].unsqueeze(3), [128, NT, 4, 4]), ALU.mult))
                chain(dv.tensor_reduce(ep[:, :, 0:4], prod[:, :, :].rearrange("p t (g j) -> p t j g", g=4),
                                       axis=AX.X, op=ALU.add))
                for t in range(NT):
                    ins = dv.max(top[:, t, :], ep[:, t, :])
                chain(ins)
                dv.tensor_tensor(td[:, :], top[:, :, 1], top[:, :, 0], ALU.subtract).then_inc(s_td, 1)
                for t in range(NT):
                    ins = dv.max_index(topi[:, t, :], top[:, t, :], ep[:, t, :])
                chain(ins)
                for q in range(2):
                    chain(dv.tensor_copy(enum[:, q, :], topi[:, :, q]))
                    chain(dv.scalar_tensor_tensor(out=enum[:, q, :], in0=gnum[:, :], scalar=4.0, in1=enum[:, q, :],
                                                  op0=ALU.mult, op1=ALU.add))
                    chain(dv.tensor_tensor(one_e[:, q, :, :], bc(iota.unsqueeze(1), [128, NT, 16]),
                                           bc(enum[:, q, :].unsqueeze(2), [128, NT, 16]), ALU.is_equal))
                dv.tensor_tensor(sel[:, :, :], one_e[:, 0, :, :], one_e[:, 1, :, :], ALU.add).then_inc(s_sel, 1)
                dv.wait_ge(s_cnt, 1)
                before = bank[3][:, 0:64].rearrange("p (t c) -> p t c", t=NT)
                for q in range(2):
                    chain(dv.tensor_tensor(prod[:, :, :], before, one_e[:, q, :, :], ALU.mult))
                    chain(dv.tensor_reduce(pos[:, q, :], prod[:, :, :], axis=AX.X, op=ALU.add))
                    chain(dv.scalar_tensor_tensor(out=pos[:, q, :], in0=enum[:, q, :], scalar=float(SEQ),
                                                  in1=pos[:, q, :], op0=ALU.mult, op1=ALU.add))
                    dv.tensor_copy(row_i[:, q, :], pos[:, q, :]).then_inc(s_row, 1)
                chain(dv.tensor_reduce(tmpr[:, 0:1], bank[3][:, 64:80], axis=AX.X, op=ALU.max))
                chain(dv.tensor_scalar(tmpr[:, 1:4], const("limits"), tmpr[:, 0:1], None, ALU.is_lt))
                chain(dv.tensor_reduce(tmpr[:, 0:1], tmpr[:, 1:4], axis=AX.X, op=ALU.add))
                dv.tensor_scalar(rounds_i[:, :], tmpr[:, 0:1], 1.0, None, ALU.add).then_inc(s_known, 1)
                dv.wait_ge(s_known, 1)
                dv.sem_inc(s_rounds, 1)
                dv.wait_ge(s_gex, 1)
                chain(dv.tensor_reduce(gw[:, :], gexp[:, :, :], axis=AX.X, op=ALU.add))
                chain(dv.reciprocal(gw[:, :], gw[:, :]))
                dv.wait_ge(s_te, 1)
                chain(dv.tensor_scalar(td[:, :], te[:, :], 1.0, None, ALU.add))
                chain(dv.reciprocal(td[:, :], td[:, :]))
                chain(dv.tensor_tensor(wtok[:, 0, :], td[:, :], gw[:, :], ALU.mult))
                chain(dv.tensor_tensor(wtok[:, 1, :], wtok[:, 0, :], te[:, :], ALU.mult))
                dv.wait_ge(s_tabt, 1)
                chain(dv.tensor_copy(pair_f[:, :], bank[6][:, 0:64]))
                dv.tensor_copy(slot_pair[:, :], pair_f[:, :])
                chain(dv.tensor_scalar(tok_f[:, :], pair_f[:, :], float(SEQ), -float(SEQ), ALU.is_ge, ALU.mult))
                dv.tensor_tensor(slot_tok[:, :], tok_f[:, :], pair_f[:, :], ALU.add).then_inc(s_slot, 1)

                dv.wait_ge(s_known, 1)
                rounds = rounds_of(dv)
                with dv.Fori(0, rounds) as r:
                    p2 = dv.snap(passes, min_val=0, max_val=NT * DEPTH)
                    base_p = dv.snap(layer * U_ATT + U_ATT + p2 * U_PASS)
                    for n in range(3):
                        make_lo(dv, base_p, n)

                    def rows_lo(i, count):
                        dv.wait_ge(s_xgh, count)
                        for q in range(2):
                            ins = dv.tensor_tensor(xgT_lo[:, i, 4 * q:4 * q + 4, :],
                                                   bank[4 + q][:, :].rearrange("p (k c) -> p k c", k=4),
                                                   xgT_hi[:, i, 4 * q:4 * q + 4, :].bitcast(f32), ALU.subtract)
                        ins.then_inc(s_xgl, 1)

                    def hidden(m, i):
                        dv.wait_ge(s_sil, m)
                        dv.tensor_tensor(hid[:, :], bank[(1, 7)[1 - i]][:, :], sil[:, :], ALU.mult).then_inc(s_hid, 1)

                    def hidden_lo(m):
                        dv.wait_ge(s_hth, m)
                        dv.tensor_tensor(hidT_lo[:, :, :], bank[4][:, :].rearrange("p (k c) -> p k c", k=4),
                                         hidT_hi[:, :, :].bitcast(f32), ALU.subtract).then_inc(s_htl, 1)

                    def step(m, i, base_e, n0, last=False, aside=False):
                        hidden(m, i)
                        make_lo(dv, base_e, n0 + 3, aside)
                        hidden_lo(m)
                        for n in range(4, 12):
                            make_lo(dv, base_e, n0 + n, aside)
                        if not last:
                            rows_lo(1 - i, m + 2)
                        for n in range(3):
                            make_lo(dv, base_e, n0 + U_E + n, aside)

                    rows_lo(0, 1)
                    for n in range(3, U_FIRST):
                        make_lo(dv, base_p, n)
                    rows_lo(1, 2)
                    for n in range(3):
                        make_lo(dv, base_p, U_FIRST + n)

                    def turn(pair, aside):
                        base_e = dv.snap(base_p + pair * (2 * U_E))
                        for k in range(2):
                            step(held(dv, pair * 2 + (k + 1)), (k + 1) % 2, base_e, U_FIRST + U_E * k, aside=aside)

                    turns(dv, turn)
                    end = dv.snap(base_p + PAIRS * 2 * U_E)
                    step(E_N - 1, 1, end, U_FIRST, last=True)
                    hidden(E_N, 0)
                    make_lo(dv, end, U_FIRST + U_E + 3)
                    hidden_lo(E_N)
                    dv.wait_ge(s_htl, E_N)
                    meet(dv, p2)
                    dv.reg_add(passes, passes, 1)
            for t in range(NT):
                combine(16 * DEPTH, t)

        @block.tensor
        def _(pe):
            pe.sem_inc(s_used, NW)
            pe.wait_ge(s_first_c, 16)
            passes = pe.alloc_register("pe_passes")
            pe.reg_mov(passes, 0)

            def three(dst, l_hi, l_lo, r_hi, r_lo, start, stop):
                pe.matmul(dst, l_hi, r_hi, start=start, stop=False)
                pe.matmul(dst, l_hi, r_lo, start=False, stop=False)
                return pe.matmul(dst, l_lo, r_hi, start=False, stop=stop)

            def group(src_hi, src_lo, n, j, t, b):
                for kk in range(2):
                    k = 2 * j + kk
                    ins = three(bank[b][:, :], src_hi[:, k, 128 * t:128 * t + 128],
                                src_lo[:, k, 128 * t:128 * t + 128],
                                w_hi[:, n % NW, 512 * kk:512 * kk + 512], w_lo[:, n % NW, 512 * kk:512 * kk + 512],
                                start=k == 0, stop=k == KT - 1)
                return ins

            def rows(src_hi, src_lo, base, n, j, banks, done=None, only=None, split=None):
                tiles = range(len(banks)) if only is None else [only]
                for t in tiles:
                    if t == 0:
                        pe.wait_ge(s_lo, base + n + 1 + NS)
                    if split is not None:
                        pe.wait_ge(s_trl, split[t])
                    ins = group(src_hi, src_lo, n, j, t, banks[t])
                    if t == len(banks) - 1:
                        ins.then_inc(s_used, 1)
                        if j == 3 and done is not None:
                            pe.wait_ge(s_used, base + n + 1 + NW)
                            pe.sem_inc(done, 1)
                    elif j == 3 and done is not None:
                        ins.then_inc(done, 1)

            def turn(src, b, s, cols=4):
                for q in range(cols):
                    ins = pe.transpose(bank[b][:, 128 * q:128 * q + 128], src(q), ident)
                ins.then_inc(s, 1)

            with pe.Fori(0, DEPTH) as layer:
                p = pe.snap(passes, min_val=0, max_val=NT * DEPTH)
                base = pe.snap(layer * U_ATT + p * U_PASS)
                for j in range(4):
                    pe.wait_ge(s_hm, j // 2 + 1)
                    turn(lambda q: mem_rows[:, j // 2, 512 * (j % 2) + 128 * q:512 * (j % 2) + 128 * q + 128], j, s_tr)
                pe.wait_ge(s_trl, 4)
                rows(mT_hi, mT_lo, base, 0, 0, (4, 5))
                for k in range(4):
                    if k < 3:
                        rows(mT_hi, mT_lo, base, k + 1, k + 1, (4, 5))
                    if k == 2:
                        pe.wait_ge(s_used, base + 4 + NW)
                        pe.sem_inc(s_mkv, 1)
                    pe.wait_ge(s_h1, k + 1)
                    for j in (2 * k, 2 * k + 1):
                        if j >= 6:
                            pe.wait_ge(s_trl, 4 + j - 5)
                        turn(lambda q: act[:, k, 512 * (j % 2) + 128 * q:512 * (j % 2) + 128 * q + 128],
                             (6, 7, 0, 1, 2, 3, 6, 7)[j], s_tr)

                def project(n):
                    if n == 1:
                        pe.wait_ge(s_mkve, 2)
                    if n >= 2:
                        pe.wait_ge(s_pev, 4 * (n - 1))
                    for j in range(4):
                        rows(hT_hi, hT_lo, base, 4 + 4 * n + j, j, tuple(range(4 * (n % 2), 4 * (n % 2) + 4)),
                             split=(8, 8, 10, 12) if n == j == 0 else None,
                             done=s_proj)

                for n in range(3):
                    project(n)
                rows(hT_hi, hT_lo, base, 16, 0, (4, 5, 6, 7))
                pe.wait_ge(s_pev, 12)
                pe.wait_ge(s_qn, 1)
                for g in range(2):
                    for t in range(2):
                        ins = pe.transpose(bank[0][:, 256 * g + 128 * t:256 * g + 128 * t + 128],
                                           ck[:, t, 128 * g:128 * g + 128], ident)
                ins.then_inc(s_tq, 1)
                for j in range(1, 7):
                    src, off = ((pq[4], 256), (pq[3], 0), (pq[3], 256))[(j - 1) // 2]
                    if j >= 4:
                        pe.wait_ge(s_tqe, j - 3)
                    turn(lambda q: src[:, q, off + 128 * ((j - 1) % 2):off + 128 * ((j - 1) % 2) + 128],
                         j % 4, s_tq)
                pe.wait_ge(s_tqe, 7)

                def scores(j):
                    t, q = j // 6, j % 6
                    if j >= 2:
                        pe.wait_ge(s_exp, j - 1)
                    tok = slice(128 * t, 128 * t + 128)
                    if q < 2:
                        for g in range(2):
                            part_ = slice(64 * q, 64 * q + 64)
                            ins = pe.matmul(bank[j % 2][:, 256 * g:256 * g + 256], hd[part_, 0, g, tok],
                                            ckT[part_, g, :], start=True, stop=True)
                    else:
                        h = q - 2
                        part_ = slice(64 * (h % 2), 64 * (h % 2) + 64)
                        ins = pe.matmul(bank[j % 2][:, 0:128 * (t + 1)], hd[part_, 1, h // 2, tok],
                                        hd[part_, 2, h // 2, 0:128 * (t + 1)], start=True, stop=True)
                    ins.then_inc(s_s, 1)

                def turn_probs(j):
                    pe.wait_ge(s_exp, j + 1)
                    if j >= 1:
                        pe.wait_ge(s_pte, j)
                    turn(lambda q: probs[:, j % 2, 128 * q:128 * q + 128], 2, s_pt,
                         cols=4 if j % 6 < 2 else j // 6 + 1)

                def values(j):
                    t, q = j // 6, j % 6
                    pe.wait_ge(s_pte, j + 1)
                    if q == 0 and t >= 1:
                        pe.wait_ge(s_yev, t)
                    o = bank[3]
                    if q < 2:
                        for g in range(2):
                            h = q + 2 * g
                            for k in range(2):
                                ins = pe.matmul(o[:, 256 + 64 * h:320 + 64 * h],
                                                probsT[:, j % 2, 256 * g + 128 * k:256 * g + 128 * k + 128],
                                                cv[:, k, 64 * h:64 * h + 64], start=k == 0, stop=k == 1)
                    else:
                        h = q - 2
                        for k in range(t + 1):
                            ins = pe.matmul(o[:, 64 * h:64 * h + 64], probsT[:, j % 2, 128 * k:128 * k + 128],
                                            pq[4][:, k, 64 * h:64 * h + 64], start=k == 0, stop=k == t)
                    ins.then_inc(s_pv, 1)

                g = 4
                for s in range(26):
                    if s < 24:
                        scores(s)
                    if 1 <= s <= 24:
                        turn_probs(s - 1)
                    if s >= 2:
                        values(s - 2)
                    for _ in range(AFTER_STEP[s]):
                        if g == 16:
                            pe.wait_ge(s_pev, 16)
                        rows(hT_hi, hT_lo, base, 16 + g // 4, g // 4 % 4, (4, 5, 6, 7), s_proj, only=g % 4)
                        g += 1
                pe.wait_ge(s_yev, 4)
                pe.wait_ge(s_rot, 1)
                for j in range(4):
                    turn(lambda q: pq[0][:, q, 128 * j:128 * j + 128], j, s_tq)
                pe.wait_ge(s_kd, 2)
                pe.wait_ge(s_pev, 20)
                for h in range(H):
                    half = slice(64 * (h % 2), 64 * (h % 2) + 64)
                    for t in range(2):
                        ins = pe.matmul(bank[4][half, 128 * (h // 2):128 * (h // 2) + 128],
                                        kd[:, t, 64 * h:64 * h + 64], pq[1][:, t, 128 * h:128 * h + 128],
                                        start=t == 0, stop=t == 1)
                ins.then_inc(s_r, 1)
                pe.wait_ge(s_tqe, 11)

                def ret_scores(r):
                    c, h = r // 4, r % 4
                    half = slice(64 * (h % 2), 64 * (h % 2) + 64)
                    if r >= 2:
                        pe.wait_ge(s_stm, r - 1)
                    pe.matmul(bank[r % 2][:, 0:256], hd[half, 1, h // 2, 256 * c:256 * c + 128],
                              hd[half, 0, h // 2, 256 * c:256 * c + 256], start=True, stop=True)
                    pe.matmul(bank[r % 2][:, 256:384], hd[half, 1, h // 2, 256 * c + 128:256 * c + 256],
                              hd[half, 0, h // 2, 256 * c + 128:256 * c + 256], start=True, stop=True)\
                        .then_inc(s_st, 1)

                def ret_values(r):
                    c, h = r // 4, r % 4
                    pe.wait_ge(s_stm, r + 1)
                    if r == 4:
                        pe.wait_ge(s_re, 1)
                        pe.wait_ge(s_qd, 1)
                    for tt in range(2):
                        t = 2 * c + tt
                        o = bank[(2, 3, 6, 7)[t]][:, 128 * h:128 * h + 128]
                        parts = [(probs[:, r % 2, 128 * tt:128 * tt + 128], pq[1][:, 2 * c, 128 * h:128 * h + 128])]
                        if tt:
                            parts.append((probs[:, r % 2, 256:384], pq[1][:, 2 * c + 1, 128 * h:128 * h + 128]))
                        if c:
                            parts.append((qdT[:, h // 2, 128 * tt:128 * tt + 128],
                                          state[:, h // 2, 128 * (h % 2):128 * (h % 2) + 128]))
                        for q, (l, rr) in enumerate(parts):
                            ins = pe.matmul(o, l, rr, start=q == 0, stop=q == len(parts) - 1)
                    ins.then_inc(s_ro, 1)

                for r in range(9):
                    if r < 8:
                        ret_scores(r)
                    if r >= 1:
                        ret_values(r - 1)
                for j in range(8):
                    t = j // 2
                    pe.wait_ge(s_yr, t + 1)
                    if j >= 4:
                        pe.wait_ge(s_trl, 12 + j - 3)
                    turn(lambda q: act[:, t, 512 * (j % 2) + 128 * q:512 * (j % 2) + 128 * q + 128],
                         (0, 1, 4, 5)[j % 4], s_tr)
                for n in range(2):
                    for j in range(4):
                        rows(hT_hi, hT_lo, base, 24 + 4 * n + j, j, ((2, 3, 6, 7), (0, 1, 4, 5))[n], s_wo,
                             split=(14, 16, 18, 20) if n == j == 0 else None)
                for j in range(8):
                    pe.wait_ge(s_h2, j // 2 + 1)
                    turn(lambda q: act[:, j // 2, 512 * (j % 2) + 128 * q:512 * (j % 2) + 128 * q + 128],
                         (2, 3, 6, 7, 0, 1, 4, 5)[j], s_tr)
                pe.wait_ge(s_wrl, 1)
                for half in range(2):
                    pe.wait_ge(s_trl, 24 + 4 * half)
                    c = slice(256 * half, 256 * half + 256)
                    for k in range(KT):
                        for part_ in ("all", "hi") if k == 0 else ("hi", "all"):
                            if part_ == "all":
                                ins = pe.matmul(bank[2 + half][0:40, c], wr_s[:, k, :], hT_hi[:, k, c],
                                                start=k == 0, stop=k == KT - 1)
                            else:
                                pe.matmul(bank[2 + half][0:20, c], wr_s[:, k, 0:20], hT_lo[:, k, c],
                                          start=False, stop=False)
                    ins.then_inc(s_lgt, 1)
                pe.wait_ge(s_lgc, 2)
                for t in range(NT):
                    ins = pe.transpose(bank[6][:, 40 * t:40 * t + 40], lgT[:, 128 * t:128 * t + 128],
                                       ident[0:40, 0:40])
                ins.then_inc(s_lg, 1)
                pe.wait_ge(s_cb, 2)
                pe.wait_ge(s_sel, 1)
                for t in range(NT):
                    for j in range(t + 1):
                        pe.matmul(bank[3][:, 16 * t:16 * t + 16], below_b[:, :] if j == t else ones_b[:, :],
                                  sel[:, j, :], start=j == 0, stop=j == t)
                for j in range(NT):
                    ins = pe.matmul(bank[3][:, 64:80], ones_b[:, :], sel[:, j, :], start=j == 0, stop=j == NT - 1)
                ins.then_inc(s_cnt, 1)
                pe.wait_ge(s_tabr, layer * 16 + 16)
                apart(pe)
                pe.transpose(bank[6][:, 0:64], tab[:, :], ident[0:64, 0:64]).then_inc(s_tabt, 1)

                pe.wait_ge(s_known, 1)
                rounds = rounds_of(pe)
                with pe.Fori(0, rounds) as r:
                    p2 = pe.snap(passes, min_val=0, max_val=NT * DEPTH)
                    base_p = pe.snap(layer * U_ATT + U_ATT + p2 * U_PASS)

                    def turn_rows(i, loaded):
                        pe.wait_ge(s_xg[i], loaded)
                        for k in range(KT):
                            ins = pe.transpose(bank[4 + k // 4][:, 128 * (k % 4):128 * (k % 4) + 128],
                                               xg[:, i, 128 * k:128 * k + 128], ident)
                        ins.then_inc(s_xgt, 1)

                    def gate_up(i, base_e, n, first, count):
                        for k8 in range(first, first + count):
                            m = n + k8 - first
                            pe.wait_ge(s_lo, base_e + (m + 1 + NS))
                            for kk in range(2):
                                k = 2 * (k8 // 2) + kk
                                ins = three(bank[(0, 6)[i] + k8 % 2][:, :], xgT_hi[:, i, k, :], xgT_lo[:, i, k, :],
                                            w_hi[:, m % NW, 512 * kk:512 * kk + 512],
                                            w_lo[:, m % NW, 512 * kk:512 * kk + 512], start=k == 0, stop=k == KT - 1)
                            ins.then_inc(s_used, 1)

                    def turn_hidden(m):
                        pe.wait_ge(s_hid, m)
                        for q in range(FT):
                            ins = pe.transpose(bank[4][:, 128 * q:128 * q + 128], hid[:, 128 * q:128 * q + 128], ident)
                        ins.then_inc(s_ht, 1)

                    def down(m, base_e, n):
                        pe.wait_ge(s_htl, m)
                        pe.wait_ge(s_ye, m)
                        for k in range(FT):
                            pe.wait_ge(s_lo, base_e + (n + k + 1 + NS))
                            for q in range(2):
                                ins = three(bank[2 + q][:, :], hidT_hi[:, k, :], hidT_lo[:, k, :],
                                            w_hi[:, (n + k) % NW, 512 * q:512 * q + 512],
                                            w_lo[:, (n + k) % NW, 512 * q:512 * q + 512], start=k == 0,
                                            stop=k == FT - 1)
                            ins.then_inc(s_used, 1)
                        pe.wait_ge(s_used, base_e + (n + FT + NW))
                        pe.sem_inc(s_y, 1)

                    def gate_up_done(base_e, n):
                        pe.wait_ge(s_used, base_e + (n + NW))
                        pe.sem_inc(s_gu, 1)

                    def step(m, i, base_e, n0, loaded, last=False):
                        pe.wait_ge(s_xgl, m + 1)
                        gate_up(i, base_e, n0, 0, 2)
                        turn_hidden(m)
                        gate_up(i, base_e, n0 + 2, 2, 2)
                        down(m, base_e, n0 + 4)
                        gate_up(i, base_e, n0 + 8, 4, 2)
                        if not last:
                            turn_rows(1 - i, loaded)
                        gate_up(i, base_e, n0 + 10, 6, 2)
                        gate_up_done(base_e, n0 + U_E)

                    turn_rows(0, p2 * 128 + 16)
                    pe.wait_ge(s_xgl, 1)
                    gate_up(0, base_p, 0, 0, 6)
                    turn_rows(1, p2 * 128 + 16)
                    gate_up(0, base_p, 6, 6, 2)
                    gate_up_done(base_p, U_FIRST)
                    with pe.Fori(0, PAIRS) as pair:
                        base_e = pe.snap(base_p + pair * (2 * U_E))
                        for k in range(2):
                            step(pe.snap(pair * 2 + (k + 1)), (k + 1) % 2, base_e, U_FIRST + U_E * k,
                                 p2 * 128 + pair * 16 + 32)
                    end = pe.snap(base_p + PAIRS * 2 * U_E)
                    step(E_N - 1, 1, end, U_FIRST, None, last=True)
                    turn_hidden(E_N)
                    down(E_N, end, U_FIRST + U_E)
                    pe.wait_ge(s_y, E_N)
                    meet(pe, p2)
                    pe.reg_add(passes, passes, 1)


_INS = ["x", "mem", "norm1_g", "w_in", "ret_norm_g", "moba_qn_g", "moba_kn_g", "mem_norm_g", "w_mem_kv", "mem_qn_g",
        "mem_kn_g", "w_out", "norm2_g", "w_router_grp", "b_router_grp", "w_router_exp", "b_router_exp", "w_exp_gate",
        "w_exp_up", "w_exp_down"]


def _constants():
    import numpy as np
    c = np.zeros((128, N_CONST), np.float32)

    def put(name, v):
        v = np.asarray(v, np.float32)
        c[:v.shape[0], OFF[name]:OFF[name] + CONST[name]] = v.reshape(v.shape[0], -1)

    f = np.float32
    p = np.arange(128)
    put("ident", np.eye(128))
    inv = (f(1.0) / (f(10000.0) ** np.linspace(0, 1, 32, dtype=f))).astype(f)
    ang = (np.arange(SEQ, dtype=f)[:, None] * inv[None, :]).astype(f)
    for name, fn in (("cos", np.cos), ("sin", np.sin)):
        put(name, fn(ang).astype(f).reshape(NT, 128, 32).transpose(1, 0, 2))
    log_g = np.log1p(-(f(2.0) ** (f(-5.0) - np.arange(H, dtype=f)))).astype(f)
    n = np.arange(256, dtype=f)
    k_scale = f(DH ** -0.5)
    diff = n[None, :] - p[:, None].astype(f)
    put("dmask", np.stack([np.where(diff >= 0, np.exp(log_g[h] * np.maximum(diff, f(0))), 0) * k_scale
                           for h in range(H)], 1))
    q_decay = np.exp(log_g[:, None] * (n + f(1)))
    put("qdec", np.stack([np.repeat(q_decay[2 * g:2 * g + 2], 64, 0) for g in range(2)], 1))
    k_decay = np.exp(log_g[:, None] * (f(255) - n)) * k_scale
    put("kdec", k_decay.reshape(H, 2, 128).transpose(2, 1, 0))
    put("causal", np.where(p[None, :] <= p[:, None], 0.0, NEG))
    put("below", p[:, None] < p[None, :])
    put("iota", np.tile(np.arange(16), (128, 1)))
    put("pairid", p[:, None] + 128 * np.arange(2 * NT)[None, :])
    put("empty", np.full((64, 128), EMPTY))
    put("limits", np.tile(128 * np.arange(1, NT), (128, 1)))
    put("eps", np.full((128, 1), 1e-6))
    return c


def kernel(**inputs):
    import numpy as _np
    import concourse.bacc as _bacc
    from concourse import mybir as _mybir
    from concourse.bass_utils import run_bass_kernel_spmd as _run

    nc = _bacc.Bacc("TRN2", target_bir_lowering=False, num_devices=1)
    arrays, args = {}, {}
    given = {name: _np.ascontiguousarray(inputs[name]) for name in _INS}
    given["const_pack"] = _constants()
    for name, arr in given.items():
        arrays[f"in_{name}"] = arr
        args[name] = nc.dram_tensor(f"in_{name}", arr.shape, _mybir.dt.from_np(arr.dtype), kind="ExternalInput").ap()
    out = nc.dram_tensor("out_x", (1, SEQ, D), _mybir.dt.float32, kind="ExternalOutput").ap()
    build(nc, args, out)
    r = _run(nc, [arrays], core_ids=[0])
    return r.results[0]["out_x"]
```
